# Optimizing a Trainium2 kernel written in Bass

```python
import jax, jax.numpy as jnp
from jax import lax
import numpy as np

D_MODEL = 1024
BATCH = 1
SEQ = 2048
DEPTH = 1
DEC_BATCH = 1
DEC_SEQ = 32
PAST_LEN = 1024

CHUNK = 64
WINDOW = 128
WIN_CHUNKS = WINDOW // CHUNK
HEAD_DIM = 64
ATTN_WIDTH = D_MODEL // 2
N_HEADS = ATTN_WIDTH // HEAD_DIM
KV_HEADS = 2
GROUP = N_HEADS // KV_HEADS
KV_WIDTH = KV_HEADS * HEAD_DIM
LRU_WIDTH = D_MODEL // 2
LRU_HEADS = 8
LRU_BLOCK = LRU_WIDTH // LRU_HEADS
CONV_WIDTH = 4
RG_C = 8.0
MIX_WIDTH = ATTN_WIDTH + LRU_WIDTH
IN_COLS = ATTN_WIDTH + 2 * KV_WIDTH + 2 * LRU_WIDTH
D_FF = 4 * D_MODEL
EPS = 1e-6
NEG = -1e30

kernel_name = "hybrid_swa_sink_rglru_stream_step"

def rmsnorm(x, g):
    xf = x.astype(jnp.float32)
    y = xf * lax.rsqrt(jnp.mean(xf * xf, axis=-1, keepdims=True) + EPS) * g.astype(jnp.float32)
    return y.astype(x.dtype)

def sink_attend(q, k, v, mask, sinks):
    logits = jnp.einsum('bnqkgd,bnskd->bnkgqs', q, k).astype(jnp.float32) * (HEAD_DIM ** -0.5)
    logits = jnp.where(mask[None, :, None, None], logits, NEG)
    sink = jnp.broadcast_to(sinks.astype(jnp.float32).reshape(1, 1, KV_HEADS, GROUP, 1, 1),
                            logits.shape[:-1] + (1,))
    probs = jax.nn.softmax(jnp.concatenate([logits, sink], axis=-1), axis=-1)[..., :-1]
    out = jnp.einsum('bnkgqs,bnskd->bnqkgd', probs.astype(v.dtype), v)
    b, n, qn = out.shape[:3]
    return out.reshape(b, n * qn, ATTN_WIDTH)

def attn_prompt(q, k, v, sinks):
    b, t = q.shape[:2]
    n_c = t // CHUNK
    qb = q.reshape(b, n_c, CHUNK, KV_HEADS, GROUP, HEAD_DIM)
    kb = k.reshape(b, n_c, CHUNK, KV_HEADS, HEAD_DIM)
    vb = v.reshape(b, n_c, CHUNK, KV_HEADS, HEAD_DIM)

    def band(xb):
        parts = [jnp.pad(xb, ((0, 0), (o, 0), (0, 0), (0, 0), (0, 0)))[:, :n_c]
                 for o in range(WIN_CHUNKS - 1, -1, -1)]
        return jnp.concatenate(parts, axis=2)

    c = jnp.arange(n_c)
    off = WIN_CHUNKS - 1 - jnp.arange(WINDOW) // CHUNK
    mask = (c[:, None] >= off[None, :])[:, None, :]
    out = sink_attend(qb, band(kb), band(vb), mask, sinks)
    return out, k[:, -WINDOW:], v[:, -WINDOW:]

def attn_sample(q, k, v, ck, cv, sinks):
    b, t = q.shape[:2]
    kk = jnp.concatenate([ck.astype(k.dtype), k], axis=1)
    vv = jnp.concatenate([cv.astype(v.dtype), v], axis=1)
    qpos = PAST_LEN + jnp.arange(t)
    kpos = PAST_LEN - WINDOW + jnp.arange(WINDOW + t)
    cq = (qpos // CHUNK)[:, None]
    ckk = (kpos // CHUNK)[None, :]
    mask = ((ckk <= cq) & (ckk > cq - WIN_CHUNKS))[None]
    qb = q.reshape(b, 1, t, KV_HEADS, GROUP, HEAD_DIM)
    out = sink_attend(qb, kk[:, None], vv[:, None], mask, sinks)
    return out, kk[:, -WINDOW:], vv[:, -WINDOW:]

def _lin_combine(e1, e2):
    a1, b1 = e1
    a2, b2 = e2
    return a1 * a2, a2 * b1 + b2

def rglru_branch(u, conv_prev, h_prev, conv_w, conv_b, wa, ba, wx, bx, lam):
    b, t = u.shape[:2]
    upad = jnp.concatenate([conv_prev.astype(u.dtype), u], axis=1)
    xc = conv_b + sum(conv_w[j] * upad[:, j:j + t] for j in range(CONV_WIDTH))
    new_conv = upad[:, -(CONV_WIDTH - 1):]
    xh = xc.reshape(b, t, LRU_HEADS, LRU_BLOCK)
    r = jax.nn.sigmoid(jnp.einsum('bthi,hij->bthj', xh, wa).reshape(b, t, LRU_WIDTH) + ba)
    i = jax.nn.sigmoid(jnp.einsum('bthi,hij->bthj', xh, wx).reshape(b, t, LRU_WIDTH) + bx)
    log_a = -RG_C * r.astype(jnp.float32) * jax.nn.softplus(-lam.astype(jnp.float32))
    a = jnp.exp(log_a)
    bt = jnp.sqrt(-jnp.expm1(2.0 * log_a)) * (i * xc).astype(jnp.float32)
    bt = bt.at[:, 0].add(a[:, 0] * h_prev.astype(jnp.float32))
    _, h = lax.associative_scan(_lin_combine, (a, bt), axis=1)
    return h.astype(u.dtype), new_conv, h[:, -1].astype(h_prev.dtype)

def block(x, cache_k, cache_v, conv_prev, h_prev, norm_mix_g, w_in, attn_sinks, conv_w, conv_b,
          gate_a_w, gate_a_b, gate_x_w, gate_x_b, lru_lambda, w_out, norm_ffn_g, w_up, w_down, prompt):
    b, t = x.shape[:2]
    xn = rmsnorm(x, norm_mix_g)
    z = xn @ w_in
    o1 = ATTN_WIDTH
    o2 = o1 + KV_WIDTH
    o3 = o2 + KV_WIDTH
    o4 = o3 + LRU_WIDTH
    q = z[..., :o1].reshape(b, t, KV_HEADS, GROUP, HEAD_DIM)
    k = z[..., o1:o2].reshape(b, t, KV_HEADS, HEAD_DIM)
    v = z[..., o2:o3].reshape(b, t, KV_HEADS, HEAD_DIM)
    u = z[..., o3:o4]
    gt = z[..., o4:]
    if prompt:
        attn_out, nk, nv = attn_prompt(q, k, v, attn_sinks)
    else:
        attn_out, nk, nv = attn_sample(q, k, v, cache_k, cache_v, attn_sinks)
    lru_h, nconv, nh = rglru_branch(u, conv_prev, h_prev, conv_w, conv_b,
                                     gate_a_w, gate_a_b, gate_x_w, gate_x_b, lru_lambda)
    lru_out = jax.nn.gelu(gt, approximate=True) * lru_h
    h = x + jnp.concatenate([attn_out, lru_out], axis=-1) @ w_out
    hn = rmsnorm(h, norm_ffn_g)
    y = h + jnp.square(jax.nn.relu(hn @ w_up)) @ w_down
    return y, nk, nv, nconv, nh

def setup_inputs(seed: int = 0) -> dict:
    key = jax.random.key(seed)
    ks = jax.random.split(key, 24)
    f = jnp.float32
    nrm = lambda k, s, sc: jax.random.normal(k, s, f) * sc
    a0 = jax.random.uniform(ks[13], (DEPTH, LRU_WIDTH), f, 0.9, 0.999)
    sa = a0 ** (1.0 / RG_C)
    lam = jnp.log(sa) - jnp.log1p(-sa)
    return {
        "x_prompt": nrm(ks[0], (BATCH, SEQ, D_MODEL), 1.0),
        "x_sample": nrm(ks[1], (DEC_BATCH, DEC_SEQ, D_MODEL), 1.0),
        "cache_k": nrm(ks[2], (DEPTH, DEC_BATCH, WINDOW, KV_HEADS, HEAD_DIM), 1.0),
        "cache_v": nrm(ks[3], (DEPTH, DEC_BATCH, WINDOW, KV_HEADS, HEAD_DIM), 1.0),
        "state_conv": nrm(ks[4], (DEPTH, DEC_BATCH, CONV_WIDTH - 1, LRU_WIDTH), 1.0),
        "state_lru": nrm(ks[5], (DEPTH, DEC_BATCH, LRU_WIDTH), 0.5),
        "norm_mix_g": 1.0 + nrm(ks[6], (DEPTH, D_MODEL), 0.02),
        "w_in": nrm(ks[7], (DEPTH, D_MODEL, IN_COLS), D_MODEL ** -0.5),
        "attn_sinks": nrm(ks[8], (DEPTH, N_HEADS), 0.5),
        "conv_w": nrm(ks[9], (DEPTH, CONV_WIDTH, LRU_WIDTH), CONV_WIDTH ** -0.5),
        "conv_b": nrm(ks[10], (DEPTH, LRU_WIDTH), 0.02),
        "gate_a_w": nrm(ks[11], (DEPTH, LRU_HEADS, LRU_BLOCK, LRU_BLOCK), LRU_BLOCK ** -0.5),
        "gate_a_b": nrm(ks[12], (DEPTH, LRU_WIDTH), 0.02),
        "gate_x_w": nrm(ks[14], (DEPTH, LRU_HEADS, LRU_BLOCK, LRU_BLOCK), LRU_BLOCK ** -0.5),
        "gate_x_b": nrm(ks[15], (DEPTH, LRU_WIDTH), 0.02),
        "lru_lambda": lam,
        "w_out": nrm(ks[16], (DEPTH, MIX_WIDTH, D_MODEL), MIX_WIDTH ** -0.5),
        "norm_ffn_g": 1.0 + nrm(ks[17], (DEPTH, D_MODEL), 0.02),
        "w_up": nrm(ks[18], (DEPTH, D_MODEL, D_FF), D_MODEL ** -0.5),
        "w_down": nrm(ks[19], (DEPTH, D_FF, D_MODEL), D_FF ** -0.5),
        "final_norm_g": 1.0 + nrm(ks[20], (D_MODEL,), 0.02),
    }

def reference(x_prompt, x_sample, cache_k, cache_v, state_conv, state_lru, norm_mix_g, w_in, attn_sinks,
              conv_w, conv_b, gate_a_w, gate_a_b, gate_x_w, gate_x_b, lru_lambda, w_out, norm_ffn_g,
              w_up, w_down, final_norm_g):
    yp = x_prompt
    ys = x_sample
    kp_l, vp_l, cp_l, hp_l = [], [], [], []
    ks_l, vs_l, cs_l, hs_l = [], [], [], []
    bp = x_prompt.shape[0]
    for l in range(DEPTH):
        zc = jnp.zeros((bp, CONV_WIDTH - 1, LRU_WIDTH), x_prompt.dtype)
        zh = jnp.zeros((bp, LRU_WIDTH), state_lru.dtype)
        yp, kp, vp, cp, hp = block(yp, None, None, zc, zh, norm_mix_g[l], w_in[l], attn_sinks[l],
                                   conv_w[l], conv_b[l], gate_a_w[l], gate_a_b[l], gate_x_w[l],
                                   gate_x_b[l], lru_lambda[l], w_out[l], norm_ffn_g[l], w_up[l],
                                   w_down[l], True)
        ys, ks_, vs_, cs, hs = block(ys, cache_k[l], cache_v[l], state_conv[l], state_lru[l],
                                     norm_mix_g[l], w_in[l], attn_sinks[l], conv_w[l], conv_b[l],
                                     gate_a_w[l], gate_a_b[l], gate_x_w[l], gate_x_b[l], lru_lambda[l],
                                     w_out[l], norm_ffn_g[l], w_up[l], w_down[l], False)
        kp_l.append(kp); vp_l.append(vp); cp_l.append(cp); hp_l.append(hp)
        ks_l.append(ks_); vs_l.append(vs_); cs_l.append(cs); hs_l.append(hs)
    y_prompt = rmsnorm(yp, final_norm_g)
    y_sample = rmsnorm(ys, final_norm_g)
    return (y_prompt, y_sample,
            jnp.stack(kp_l), jnp.stack(vp_l), jnp.stack(cp_l), jnp.stack(hp_l),
            jnp.stack(ks_l), jnp.stack(vs_l), jnp.stack(cs_l), jnp.stack(hs_l))


_drawn_inputs = setup_inputs


def setup_inputs(seed=0):
    import zlib

    import numpy as np

    out = dict(_drawn_inputs(seed))
    spreads = {}
    factors = {'norm_mix_g': 2.712,
     'attn_sinks': 64.0,
     'gate_a_b': 8.0,
     'gate_x_b': 8.0,
     'norm_ffn_g': 3.241,
     'final_norm_g': 8.796}
    for name, (base, spread) in spreads.items():
        noise = np.random.default_rng([zlib.crc32(name.encode()), seed]).standard_normal(out[name].shape)
        drawn = base * np.exp(spread * noise) if base else spread * noise
        out[name] = __import__('jax').numpy.asarray(drawn.astype(out[name].dtype))
    for name, factor in factors.items():
        out[name] = (out[name] * factor).astype(out[name].dtype)
    return out
```

```python
from contextlib import ExitStack

import numpy as np
import concourse.bass as bass
from concourse import mybir

F32 = mybir.dt.float32
F32R = mybir.dt.float32r
ALU = mybir.AluOpType
ACT = mybir.ActivationFunctionType
AX_X = mybir.AxisListType.X

P = 128
D = 1024
SEQ = 2048
SAMPLE = 32
TOKENS = SEQ + SAMPLE
CHUNK = 64
WINDOW = 128
HEAD = 64
KT = D // P
FF = 4 * D
FT = FF // P
LT = 4
ATTN = 512
LRU = 512
TAPS = 4
SCALE = HEAD ** -0.5
NEG = -1e30
EPS = 1e-6

B1 = 448
NB1 = 4
FIRST = SEQ - NB1 * B1
XR, XR0 = 112, 96
B2 = 416
NB2 = TOKENS // B2
YR = 104
Z1 = 14
U1 = Z1 + 8
USES = Z1 + 16
L1 = 6
U2 = 64
L2 = 16
G1 = U1 * (NB1 + 1)
K_SAMPLE = CHUNK + FIRST

CHAIN1 = 40
V_GMIX, V_GFFN, V_CW, V_CB, V_BA, V_BX, V_LAM, V_SC, V_SL = 0, 8, 16, 32, 36, 40, 44, 48, 60
VROWS = 64


class Chain:

    def __init__(self, eng, sem):
        self.eng, self.sem, self.base, self.n = eng, sem, 0, 0

    def link(self, ins):
        ins.then_inc(self.sem, 1)
        self.n += 1
        self.eng.wait_ge(self.sem, self.base + self.n)

    def enter(self, i, stride):
        self.start, self.stride = self.n, stride
        self.base, self.n = self.start + i * stride, 0

    def leave(self, times):
        assert self.n == self.stride, (self.n, self.stride)
        self.base, self.n = 0, self.start + times * self.stride


class Block1:

    def __init__(self, b, last=False):
        self.b, self.last = b, last
        self.first = isinstance(b, int) and b == 0
        self.n = FIRST + SAMPLE if self.first else B1
        self.xr = XR0 if self.first else XR
        self.tiles = self.n // self.xr
        self.segs = [(0, 0, FIRST), (FIRST + 3, FIRST, SAMPLE)] if self.first else [(0, 0, B1)]
        if self.first:
            self.rounds = [(0, CHUNK, CHUNK, CHUNK)]
            self.rounds += [(CHUNK * c, CHUNK, CHUNK * c, WINDOW) for c in range(1, FIRST // CHUNK)]
            self.rounds += [(FIRST, SAMPLE, K_SAMPLE, CHUNK + SAMPLE)]
        else:
            self.rounds = [(CHUNK * c, CHUNK, CHUNK * c, WINDOW) for c in range(B1 // CHUNK)]

    def before(self, each, in_first=None):
        if self.first:
            return 0
        return (each if in_first is None else in_first) + (self.b - 1) * each

    def next(self):
        return None if self.last else Block1(self.b + 1)


def use_after(n):
    return n + 1 if n < Z1 else Z1 + 2 * (n - Z1 + 1)


def build_program(nc, x_prompt, x_sample, cache_k, cache_v, state_conv, state_lru, norm_mix_g, w_in, attn_sinks,
                  conv_w, conv_b, gate_a_w, gate_a_b, gate_x_w, gate_x_b, lru_lambda, w_out, norm_ffn_g, w_up,
                  w_down, final_norm_g, y_prompt, y_sample, nk_prompt, nv_prompt, nconv_prompt, nlru_prompt,
                  nk_sample, nv_sample, nconv_sample, nlru_sample):
    ctx = ExitStack()
    with ctx:
        h_dram = nc.dram_tensor("h_scratch", (P, KT, TOKENS), F32, kind="Internal").ap()

        def sb(name, shape, dt=F32):
            return ctx.enter_context(nc.sbuf_tensor(name, shape, dt))

        def sem(name):
            return ctx.enter_context(nc.semaphore(name))

        raw = sb("raw", [P, 2, 2 * D])
        w_hi = [sb(f"w_hi{s}", [P, D], F32R) for s in range(2)]
        w_lo = [sb(f"w_lo{s}", [P, D], F32R) for s in range(2)]
        ident = sb("ident", [P, P])
        ones = sb("ones", [P, P])
        vec = sb("vec", [P, VROWS])
        eps_t = sb("eps_t", [P, 1])

        phase1 = ExitStack()

        def sb1(name, shape, dt=F32):
            return phase1.enter_context(nc.sbuf_tensor(name, shape, dt))

        xrow = sb1("xrow", [P, 2, D])
        xT = sb1("xT", [P, KT, B1])
        hacc = sb1("hacc", [P, KT, B1])
        xg_hi = sb1("xg_hi", [P, KT, B1], F32R)
        xg_lo = sb1("xg_lo", [P, KT, B1], F32R)
        mix_hi = sb1("mix_hi", [P, KT, B1], F32R)
        mix_lo = sb1("mix_lo", [P, KT, B1], F32R)
        uT = sb1("uT", [P, LT, B1 + 3])
        gT = sb1("gT", [P, LT * B1])
        kT = sb1("kT", [P, CHUNK + B1])
        vT = sb1("vT", [P, CHUNK + B1])
        qT = sb1("qT", [P, 2, 2 * B1])
        xc = sb1("xc", [P, LT * B1])
        rt = sb1("rt", [P, LT * B1])
        ix = sb1("ix", [P, LT * B1])
        av = sb1("av", [P, LT * B1])
        carry = sb1("carry", [P, LT])
        vrow = sb1("vrow", [P, 7, P])
        prob = sb1("prob", [P, 2, 4, WINDOW])
        pT = sb1("pT", [P, 2, 4, P])
        sq = sb1("sq", [P, 2, B1])
        sumsq = sb1("sumsq", [P, B1])
        rstd = sb1("rstd", [P, B1])
        gate_w = sb1("gate_w", [P, 2, LT, P])
        sink8 = sb1("sink8", [P, 8])
        sink = sb1("sink", [P, 2, 4])
        sink_s = sb1("sink_s", [CHUNK, 2, 4])
        soft = sb1("soft", [P, 2, 5, 4])
        decay = sb1("decay", [P, 2, LT])
        tiny = sb1("tiny", [P, 8, LT])
        vrows = sb1("vrows", [VROWS, P])
        cache_rows = sb1("cache_rows", [CHUNK, 2, P])
        state = sb1("state", [P, 32])
        state_rows = sb1("state_rows", [32, P])
        krow = sb1("krow", [P, 2, P])
        phase1.close()

        phase2 = ExitStack()

        def sb2(name, shape, dt=F32):
            return phase2.enter_context(nc.sbuf_tensor(name, shape, dt))

        hid_hi = sb2("hid_hi", [P, FT, B2], F32R)
        hid_lo = sb2("hid_lo", [P, FT, B2], F32R)
        hn_hi = sb2("hn_hi", [P, KT, B2], F32R)
        hn_lo = sb2("hn_lo", [P, KT, B2], F32R)
        hnext = sb2("hnext", [P, KT, B2])
        hcur = sb2("hcur", [P, KT, B2])
        gfin = sb2("gfin", [P, D])
        yout = sb2("yout", [P, D])
        act_t = sb2("act_t", [P, 2, B2])
        hn_t = sb2("hn_t", [P, B2])
        sq2 = sb2("sq2", [P, B2])
        sumsq2 = sb2("sumsq2", [P, B2])
        rstd2 = sb2("rstd2", [P, B2])
        ystat = sb2("ystat", [P, 4])
        phase2.close()

        scores_a = ctx.enter_context(nc.psum_tensor("scores_a", [P, 2, 512], F32))
        banks = [ctx.enter_context(nc.psum_tensor(f"bank{b}", [P, 512], F32)) for b in (0, 1, 4, 5)]
        banks = banks[0:2] + [scores_a[:, 0, :], scores_a[:, 1, :]] + banks[2:4]
        aux = ctx.enter_context(nc.psum_tensor("aux", [P, 2, 512], F32))

        raw_in = [sem(f"raw_in{s}") for s in range(2)]
        w_hi_done, w_lo_done = sem("w_hi_done"), sem("w_lo_done")
        const_in, const_set, vec_ready = sem("const_in"), sem("const_set"), sem("vec_ready")
        vec_t, decay_e, setup_done = sem("vec_t"), sem("decay_e"), sem("setup_done")
        x_in = [sem("x_in0"), sem("x_in1")]
        xt_ready, xt_copied, x_sq, sum_done = sem("xt_ready"), sem("xt_copied"), sem("x_sq"), sem("sum_done")
        xg_hi_done, xg_lo_done = sem("xg_hi_done"), sem("xg_lo_done")
        sum_all, std_done, rstd_done = sem("sum_all"), sem("std_done"), sem("rstd_done")
        ready, freed = sem("ready"), sem("freed")
        tap0, conv_done, gates_ready, sig_done = sem("tap0"), sem("conv_done"), sem("gates_ready"), sem("sig_done")
        ix_done, tanh_done, newton, sqrt_done = sem("ix_done"), sem("tanh_done"), sem("newton"), sem("sqrt_done")
        drive, scan_in, gelu_done, mixed = sem("drive"), sem("scan_in"), sem("gelu_done"), sem("mixed")
        lru_hi, lru_lo = sem("lru_hi"), sem("lru_lo")
        vwin_ready, vwin_copied = sem("vwin_ready"), sem("vwin_copied")
        scores_ready, bound_done, exp_done = sem("scores_ready"), sem("bound_done"), sem("exp_done")
        share_done = sem("share_done")
        probs_done, pT_ready, pT_copied = sem("probs_done"), sem("pT_ready"), sem("pT_copied")
        o_ready, o_hi, o_lo = sem("o_ready"), sem("o_hi"), sem("o_lo")
        h_stored = sem("h_stored")
        halo_done = sem("halo_done")
        cache_in, cache_t, cache_copied = sem("cache_in"), sem("cache_t"), sem("cache_copied")
        state_set, state_t, state_copied = sem("state_set"), sem("state_t"), sem("state_copied")
        small_out = sem("small_out")
        dve_chain, act_chain, pool_chain = sem("dve_chain"), sem("act_chain"), sem("pool_chain")
        hnext_in, hcur_in, gfin_in = sem("hnext_in"), sem("hcur_in"), sem("gfin_in")
        sum2_done, sum2_all, std2_done = sem("sum2_done"), sem("sum2_all"), sem("std2_done")
        hn_done, hn_hi_done, hn_lo_done = sem("hn_done"), sem("hn_hi_done"), sem("hn_lo_done")
        unit_done = sem("unit_done")
        relu_done, sq_done, hid_hi_done, hid_lo_done = sem("relu_done"), sem("sq_done"), sem("hid_hi_done"), sem("hid_lo_done")
        y_done, yT_ready, ystd_done, yout_done, y_stored = sem("y_done"), sem("yT_ready"), sem("ystd_done"), sem("yout_done"), sem("y_stored")

        block = ctx.enter_context(nc.Block())

        xp, xs = x_prompt[0], x_sample[0]
        win_v = w_in[0].rearrange("(c p) n -> p c n", p=P)
        wout_lru = w_out[0, ATTN:ATTN + LRU, :].rearrange("(c p) n -> p c n", p=P)
        wout_attn = [w_out[0, kv * 256:(kv + 1) * 256, :].rearrange("(t d) n -> d t n", d=HEAD) for kv in range(2)]
        wup_v = w_up[0].rearrange("(c p) n -> p c n", p=P)
        wdown_v = w_down[0].rearrange("(k c p) n -> k p c n", p=P, c=KT)
        UNIT_COLS = [768, 1024, 1280, 1536, 512]

        def load_of1(n):
            return n // 2 if n < 20 else n - 10

        def raw_unit1(n):
            r, a = raw[:, load_of1(n) % 2, :], n % 2
            if n < 10:
                return r.rearrange("p (c n) -> p c n", c=KT)[:, :, a * P:(a + 1) * P]
            if n < Z1:
                return r.rearrange("p (c kv a d) -> p c kv a d", c=KT, kv=2, a=2)[:, :, :, a, :]
            if n < 20:
                return r.rearrange("p (c n) -> p c n", c=4)[:, :, a * 256:(a + 1) * 256]
            return r[:, 0:D].rearrange("p (c n) -> p c n", c=4)

        def raw_unit2(n):
            r, a = raw[:, (n // 2) % 2, :], n % 2
            return r.rearrange("p (c n) -> p c n", c=KT)[:, :, a * P:(a + 1) * P]

        def like_unit1(w, n):
            if n < 10:
                return w[:, :].rearrange("p (c n) -> p c n", c=KT)
            if n < Z1:
                return w[:, :].rearrange("p (c kv d) -> p c kv d", c=KT, kv=2)
            return w[:, :].rearrange("p (c n) -> p c n", c=4)

        def like_unit2(w):
            return w[:, :].rearrange("p (c n) -> p c n", c=KT)

        def scores_of(r, m):
            t = scores_a if r % 2 == 0 else aux
            return t[m, :, :].rearrange("p kv (j n) -> p (kv j) n", j=2)

        def flat(t, n):
            return t[:, 0:LT * n]

        def pair(t, n, h):
            return t[:, 2 * h * n:2 * (h + 1) * n]

        def tiles(t, n):
            return t[:, 0:LT * n].rearrange("p (j n) -> p j n", j=LT)

        @block.sync
        def _(sp):
            def load_group1(g):
                s = g % 2
                if g < 5:
                    dst, cols = raw[:, s, :].rearrange("p (c n) -> p c n", c=KT), slice(UNIT_COLS[g], UNIT_COLS[g] + 256)
                    for c in (slice(0, 4), slice(4, 8)):
                        sp.dma_start(dst[:, c, :], win_v[:, c, cols]).then_inc(raw_in[s], 16)
                elif g < 7:
                    dst = raw[:, s, :].rearrange("p (c kv n) -> p c kv n", c=KT, kv=2)
                    for kv in range(2):
                        col = kv * 256 + (g - 5) * P
                        sp.dma_start(dst[:, :, kv, :], win_v[:, :, col:col + P]).then_inc(raw_in[s], 16)
                elif g < 9:
                    dst, cols = raw[:, s, :].rearrange("p (c n) -> p c n", c=LT), slice((g - 7) * 512, (g - 6) * 512)
                    for c in (slice(0, 2), slice(2, 4)):
                        sp.dma_start(dst[:, c, :], wout_lru[:, c, cols]).then_inc(raw_in[s], 16)
                else:
                    width = 512 if g == 9 else 256
                    at = 0 if g == 9 else 512 + (g - 10) * 256
                    dst = raw[:, s, 0:4 * width].rearrange("p (c n) -> p c n", c=4)
                    for kv in range(2):
                        sp.dma_start(dst[kv * HEAD:(kv + 1) * HEAD, :, :], wout_attn[kv][:, :, at:at + width])\
                          .then_inc(raw_in[s], 16)

            def load_group2(g):
                dst = raw[:, g % 2, :].rearrange("p (c n) -> p c n", c=KT)
                if g < 16:
                    source = wup_v[:, :, g * 256:(g + 1) * 256]
                else:
                    dp, kq = (g - 16) // 4, (g - 16) % 4
                    source = wdown_v[kq][:, :, dp * 256:(dp + 1) * 256]
                for c in (slice(0, 4), slice(4, 8)):
                    sp.dma_start(dst[:, c, :], source[:, c, :]).then_inc(raw_in[g % 2], 16)

            def load_x(blk, r):
                if not blk.first:
                    rows = bass.ds(FIRST + (blk.b - 1) * B1 + r * XR, XR)
                    sp.dma_start(xrow[0:XR, r % 2, :], xp[rows, :]).then_inc(x_in[r % 2], 32)
                elif r < 2:
                    sp.dma_start(xrow[0:XR0, r, :], xp[r * XR0:(r + 1) * XR0, :]).then_inc(x_in[r], 32)
                else:
                    rest = FIRST - 2 * XR0
                    sp.dma_start(xrow[0:rest, 0, :], xp[2 * XR0:FIRST, :]).then_inc(x_in[0], 16)
                    sp.dma_start(xrow[rest:XR0, 0, :], xs[:, :]).then_inc(x_in[0], 16)

            first = Block1(0)
            load_x(first, 0)
            load_x(first, 1)
            for at, rows, source in (
                    (V_GMIX, 8, norm_mix_g[0]), (V_GFFN, 8, norm_ffn_g[0]),
                    (V_CW, 16, conv_w[0].rearrange("t n -> (t n)")), (V_CB, 4, conv_b[0]),
                    (V_BA, 4, gate_a_b[0]), (V_BX, 4, gate_x_b[0]), (V_LAM, 4, lru_lambda[0]),
                    (V_SC, 12, state_conv[0, 0].rearrange("t n -> (t n)")), (V_SL, 4, state_lru[0, 0])):
                sp.dma_start(vrows[at:at + rows, :], source.rearrange("(r p) -> r p", p=P)).then_inc(const_in, 16)
            load_group1(0)
            load_group1(1)
            sp.dma_start(sink8[:, :], attn_sinks.to_broadcast([P, 8])).then_inc(const_in, 16)
            sp.wait_ge(const_set, 1)
            for g, w in enumerate((gate_a_w, gate_x_w)):
                heads = w[0].rearrange("(j h) a b -> h a j b", h=2)
                for hh in range(2):
                    s = slice(hh * HEAD, (hh + 1) * HEAD)
                    sp.dma_start(gate_w[s, g, :, s], heads[hh]).then_inc(const_in, 16)
            sp.dma_start(cache_rows[:, 0, :], cache_k[0, 0, CHUNK:WINDOW].rearrange("s h d -> s (h d)")).then_inc(cache_in, 16)
            sp.dma_start(cache_rows[:, 1, :], cache_v[0, 0, CHUNK:WINDOW].rearrange("s h d -> s (h d)")).then_inc(cache_in, 16)
            for new, old in ((nk_sample, cache_k), (nv_sample, cache_v)):
                sp.dma_start(new[0, 0, 0:WINDOW - SAMPLE].rearrange("s h d -> s (h d)"),
                             old[0, 0, SAMPLE:WINDOW].rearrange("s h d -> s (h d)")).then_inc(small_out, 16)
            sp.wait_ge(xt_ready, 2)
            load_x(first, 2)

            def mix_block(blk):
                units, uses = blk.before(U1), blk.before(USES)
                nxt = blk.next()
                for q in range(12):
                    sp.wait_ge(w_lo_done, units + (2 * q + 2 if q < 10 else q + 11))
                    if q + 2 < 12:
                        load_group1(q + 2)
                    elif nxt:
                        load_group1(q - 10)
                    else:
                        load_group2(q - 10)
                    if nxt and q == 2:
                        load_x(nxt, 0)
                        load_x(nxt, 1)
                    if nxt and q == 9:
                        for r in (2, 3):
                            sp.wait_ge(xt_ready, nxt.before(8, 6) + 2 * (r - 2) + 2)
                            load_x(nxt, r)
                for half in range(2):
                    d = slice(4 * half, 4 * half + 4)
                    sp.wait_ge(freed, 2 + uses + Z1 + 8 + 4 * half + 4)
                    if blk.first:
                        sp.dma_start(h_dram[:, d, 0:FIRST], hacc[:, d, 0:FIRST]).then_inc(h_stored, 16)
                        sp.dma_start(h_dram[:, d, SEQ:TOKENS], hacc[:, d, FIRST:FIRST + SAMPLE]).then_inc(h_stored, 16)
                    else:
                        sp.dma_start(h_dram[:, d, bass.ds(FIRST + (blk.b - 1) * B1, B1)], hacc[:, d, :])\
                          .then_inc(h_stored, 16)

            mix_block(first)
            sp.dma_start(nk_sample[0, 0, WINDOW - SAMPLE:WINDOW].rearrange("s h d -> s (h d)"),
                         krow[CHUNK:CHUNK + SAMPLE, 0, :]).then_inc(small_out, 16)
            sp.dma_start(nv_sample[0, 0, WINDOW - SAMPLE:WINDOW].rearrange("s h d -> s (h d)"),
                         vrow[CHUNK:CHUNK + SAMPLE, 4, :]).then_inc(small_out, 16)
            with sp.Fori(1, NB1) as b:
                mix_block(Block1(b))
            mix_block(Block1(NB1, last=True))
            sp.dma_start(nk_prompt[0, 0].rearrange("s h d -> s (h d)"), krow[:, 1, :]).then_inc(small_out, 16)
            sp.dma_start(nv_prompt[0, 0].rearrange("s h d -> s (h d)"), vrow[:, 6, :]).then_inc(small_out, 16)
            sp.wait_ge(state_copied, 1)
            for dst, at, rows in ((nconv_prompt[0, 0].rearrange("t n -> (t n)"), 0, 12),
                                  (nconv_sample[0, 0].rearrange("t n -> (t n)"), 12, 12),
                                  (nlru_prompt[0, 0], 24, 4), (nlru_sample[0, 0], 28, 4)):
                sp.dma_start(dst.rearrange("(r p) -> r p", p=P), state_rows[at:at + rows, :]).then_inc(small_out, 16)
            sp.wait_ge(small_out, 10 * 16)
            sp.wait_ge(h_stored, 64 + 32 * NB1)
            sp.dma_start(hnext[:, :, :], h_dram[:, :, 0:B2]).then_inc(hnext_in, 16)
            sp.dma_start(hcur[:, :, :], h_dram[:, :, 0:B2]).then_inc(hcur_in, 16)
            sp.dma_start(gfin[:, :], final_norm_g.rearrange("(a n) -> a n", a=1).to_broadcast([P, D])).then_inc(y_stored, 16)

            def store_y(b, r, last=False):
                sp.wait_ge(yout_done, 1 + b * 4 + r + 1)
                if last and r == 3:
                    rest = YR - SAMPLE
                    sp.dma_start(y_prompt[0, SEQ - rest:SEQ, :], yout[0:rest, :]).then_inc(y_stored, 16)
                    sp.dma_start(y_sample[0], yout[rest:YR, :]).then_inc(y_stored, 16)
                else:
                    sp.dma_start(y_prompt[0, bass.ds(b * B2 + r * YR, YR), :], yout[0:YR, :]).then_inc(y_stored, 16)

            def loads(b, lo, hi, more, flush=False, ahead=False):
                for q in range(lo, hi):
                    sp.wait_ge(w_lo_done, G1 + b * U2 + 2 * q + 2)
                    if q + 2 < 32 or more:
                        load_group2((q + 2) % 32)
                    if ahead and q == 1:
                        sp.wait_ge(hn_done, 8 * b + 8)
                        sp.dma_start(hnext[:, :, :], h_dram[:, :, bass.ds((b + 1) * B2, B2)]).then_inc(hnext_in, 16)
                    if flush and 2 <= q < 6:
                        store_y(b - 1, q - 2)
                    if flush and q == 7:
                        sp.wait_ge(yT_ready, 4 * b)
                        sp.dma_start(hcur[:, :, :], h_dram[:, :, bass.ds(b * B2, B2)]).then_inc(hcur_in, 16)

            loads(0, 0, 16, True, ahead=True)
            with sp.Fori(0, NB2 - 2) as b:
                loads(b, 16, 32, True)
                loads(b + 1, 0, 16, True, flush=True, ahead=True)
            loads(NB2 - 2, 16, 32, True)
            loads(NB2 - 1, 0, 16, True, flush=True)
            loads(NB2 - 1, 16, 32, False)
            for r in range(4):
                store_y(NB2 - 1, r, last=True)
            sp.wait_ge(y_stored, 16 + 16 * (4 * NB2 + 1))

        @block.gpsimd
        def _(pool):
            nc.gpsimd.memset(gate_w[:, :, :, :], 0.0).then_inc(const_set, 1)
            nc.gpsimd.memset(ident[:, :], 0.0).then_inc(const_set, 1)
            nc.gpsimd.memset(ones[:, :], 1.0).then_inc(const_set, 1)
            pool.wait_ge(const_set, 2)
            nc.gpsimd.affine_select(out=ident[:, :], in_=ident[:, :], compare_op=ALU.not_equal, fill=1.0, base=0,
                                    pattern=[[-1, P]], channel_multiplier=1).then_inc(const_set, 1)

            def sum_squares(blk):
                sums = blk.before(7)
                for c in range(1, KT):
                    pool.wait_ge(x_sq, blk.before(8) + c + 1)
                    if c == 1:
                        nc.gpsimd.tensor_tensor(sumsq[:, 0:blk.n], sq[:, 0, 0:blk.n], sq[:, 1, 0:blk.n], ALU.add)\
                          .then_inc(sum_done, 1)
                    else:
                        pool.wait_ge(sum_done, sums + c - 1)
                        nc.gpsimd.tensor_tensor(sumsq[:, 0:blk.n], sumsq[:, 0:blk.n], sq[:, c % 2, 0:blk.n], ALU.add)\
                          .then_inc(sum_done, 1)

            def mix_block(blk):
                n = blk.n
                for h in range(2):
                    pool.wait_ge(sig_done, blk.before(8) + 4 * h + 4)
                    nc.gpsimd.tensor_tensor(pair(ix, n, h), pair(ix, n, h), pair(xc, n, h), ALU.mult).then_inc(ix_done, 1)
                for h in range(2):
                    pool.wait_ge(ix_done, blk.before(2) + h + 1)
                    pool.wait_ge(drive, blk.before(2) + h + 1)
                    nc.gpsimd.tensor_tensor(pair(ix, n, h), pair(ix, n, h), pair(rt, n, h), ALU.mult).then_inc(scan_in, 1)
                for r, (_, qn, _, nk) in enumerate(blk.rounds):
                    pool.wait_ge(share_done, blk.before(7, 5) + r + 1)
                    m = slice(0, 2 * qn)
                    share = soft[m, r % 2, 3, :].rearrange("p (a o) -> p a o", o=1).to_broadcast([2 * qn, 4, nk])
                    nc.gpsimd.tensor_tensor(prob[m, r % 2, :, :nk], prob[m, r % 2, :, :nk], share, ALU.mult).then_inc(probs_done, 1)
                if not blk.last:
                    sum_squares(blk.next())

            sum_squares(Block1(0))
            mix_block(Block1(0))
            with pool.Fori(1, NB1) as b:
                mix_block(Block1(b))
            mix_block(Block1(NB1, last=True))

            def sum_squares2(b):
                chain = b * 8
                pool.wait_ge(hnext_in, 16 * b + 16)
                for c in range(KT):
                    if c == 0:
                        nc.gpsimd.tensor_tensor(sumsq2[:, :], hnext[:, 0, :], hnext[:, 0, :], ALU.mult).then_inc(pool_chain, 1)
                        pool.wait_ge(pool_chain, chain + 1)
                    else:
                        if c > 1:
                            pool.wait_ge(sum2_done, b * 7 + c - 1)
                        nc.gpsimd.tensor_tensor(sq2[:, :], hnext[:, c, :], hnext[:, c, :], ALU.mult).then_inc(pool_chain, 1)
                        pool.wait_ge(pool_chain, chain + c + 1)
                        nc.gpsimd.tensor_tensor(sumsq2[:, :], sumsq2[:, :], sq2[:, :], ALU.add).then_inc(sum2_done, 1)

            sum_squares2(0)
            with pool.Fori(1, NB2) as b:
                sum_squares2(b)

        @block.scalar
        def _(act):
            chain = Chain(act, act_chain)

            def split1(blk, n):
                g = load_of1(n % U1)
                loads = blk.before(L1) + (L1 if n >= U1 else 0)
                act.wait_ge(raw_in[g % 2], 32 * (loads + g // 2 + 1))
                nc.scalar.activation(like_unit1(w_hi[n % 2], n % U1), raw_unit1(n % U1), ACT.Copy).then_inc(w_hi_done, 1)

            def split2(b, n):
                g = (n % U2) // 2
                loads = L1 * (NB1 + 1) + b * L2 + (L2 if n >= U2 else 0)
                act.wait_ge(raw_in[g % 2], 32 * (loads + g // 2 + 1))
                nc.scalar.activation(like_unit2(w_hi[n % 2]), raw_unit2(n % U2), ACT.Copy).then_inc(w_hi_done, 1)

            def step1(blk, n):
                act.wait_ge(ready, blk.before(USES) + use_after(n))
                if n + 2 >= U1 and blk.last:
                    split2(-1, U2 + n + 2 - U1)
                else:
                    split1(blk, n + 2)

            def copy_x(blk, r):
                for half in range(2):
                    act.wait_ge(xt_ready, blk.before(8, 6) + 2 * r + half + 1)
                    c = slice(4 * half, 4 * half + 4)
                    nc.scalar.activation(xT[:, c, r * blk.xr:(r + 1) * blk.xr],
                                         aux[:, half, 0:4 * blk.xr].rearrange("p (c n) -> p c n", c=4), ACT.Copy)\
                      .then_inc(xt_copied, 1)

            def prepare_x(blk, cs):
                n = blk.n
                for c in cs:
                    if c == 0:
                        act.wait_ge(xt_copied, blk.before(8, 6) + 2 * blk.tiles)
                    if c >= 2:
                        act.wait_ge(sum_done, blk.before(7) + max(1, c - 2))
                    nc.scalar.activation(sq[:, c % 2, 0:n], xT[:, c, 0:n], ACT.Square).then_inc(x_sq, 1)
                    nc.scalar.activation(xg_hi[:, c, 0:n], xT[:, c, 0:n], ACT.Copy, scale=vec[:, V_GMIX + c:V_GMIX + c + 1])\
                      .then_inc(xg_hi_done, 1)

            def exps(blk, r):
                _, qn, _, nk = blk.rounds[r]
                m, t = slice(0, 2 * qn), r % 2
                act.wait_ge(bound_done, blk.before(7, 5) + r + 1)
                if r >= 2:
                    act.wait_ge(pT_ready, blk.before(7, 5) + r - 1)
                for a in range(4):
                    nc.scalar.activation(prob[m, t, a, 0:nk], scores_of(r, m)[:, a, 0:nk], ACT.Exp, scale=SCALE,
                                         bias=soft[m, t, 1, a:a + 1], accum_out=soft[m, t, 2, a:a + 1])
                nc.scalar.activation(soft[m, t, 4, :], soft[m, t, 4, :], ACT.Exp).then_inc(exp_done, 1)

            def copy_pT(blk, r):
                _, qn, _, nk = blk.rounds[r]
                act.wait_ge(pT_ready, blk.before(7, 5) + r + 1)
                nc.scalar.activation(pT[0:nk, r % 2, :, 0:2 * qn],
                                     banks[4][0:nk, :].rearrange("p (a n) -> p a n", a=4)[:, :, 0:2 * qn], ACT.Copy)\
                  .then_inc(pT_copied, 1)

            def attn_high(blk, r):
                q0, qn, _, _ = blk.rounds[r]
                act.wait_ge(o_ready, blk.before(7, 5) + r + 1)
                nc.scalar.activation(mix_hi[:, 0:4, q0:q0 + qn], banks[5][:, 0:4 * qn].rearrange("p (t n) -> p t n", t=4),
                                     ACT.Copy).then_inc(o_hi, 1)

            def mix_block(blk):
                n, rounds = blk.n, len(blk.rounds)
                nxt = blk.next()
                act.wait_ge(sum_all, blk.before(1) + 1)
                nc.scalar.activation(rstd[:, 0:n], aux[:, 0, 0:n], ACT.Sqrt, scale=1.0 / D, bias=eps_t[:, 0:1])\
                  .then_inc(std_done, 1)
                for u in range(Z1):
                    step1(blk, u)
                    if u < LT:
                        act.wait_ge(freed, 2 + blk.before(USES) + u + 1)
                        for a, o, m in blk.segs:
                            nc.scalar.activation(tiles(xc, n)[:, u, o:o + m], uT[:, u, a:a + m], ACT.Identity,
                                                 scale=vec[:, V_CW + u:V_CW + u + 1],
                                                 bias=vec[:, V_CB + u:V_CB + u + 1]).then_inc(tap0, 1)
                    if 2 <= u < 6:
                        j = u - 2
                        for g, (dst, at) in enumerate(((rt, V_BA), (ix, V_BX))):
                            act.wait_ge(gates_ready, blk.before(8) + 2 * j + g + 1)
                            nc.scalar.activation(tiles(dst, n)[:, j, :], aux[:, g, 0:n], ACT.Sigmoid,
                                                 bias=vec[:, at + j:at + j + 1]).then_inc(sig_done, 1)
                    if u in (6, 7):
                        act.wait_ge(sig_done, blk.before(8) + 4 * (u - 6) + 4)
                        for j in (2 * (u - 6), 2 * (u - 6) + 1):
                            nc.scalar.activation(tiles(av, n)[:, j, :], tiles(rt, n)[:, j, :], ACT.Exp,
                                                 scale=decay[:, 0, j:j + 1]).then_inc(act_chain, 1)
                            chain.n += 1
                    if u in (7, 8):
                        act.wait_ge(act_chain, chain.base + chain.n)
                        for j in (2 * (u - 7), 2 * (u - 7) + 1):
                            nc.scalar.activation(tiles(rt, n)[:, j, :], tiles(rt, n)[:, j, :], ACT.Tanh,
                                                 scale=decay[:, 1, j:j + 1]).then_inc(tanh_done, 1)
                    if u == 9:
                        for h in range(2):
                            act.wait_ge(newton, blk.before(2) + h + 1)
                            nc.scalar.activation(pair(rt, n, h), pair(rt, n, h), ACT.Sqrt, scale=4.0).then_inc(sqrt_done, 1)
                    if u == 10:
                        nc.scalar.activation(flat(gT, n), flat(gT, n), ACT.Gelu_apprx_tanh).then_inc(gelu_done, 1)
                    if u == 11:
                        act.wait_ge(vwin_ready, blk.before(2) + 2)
                        if blk.first:
                            for r, (_, _, _, nk) in enumerate(blk.rounds):
                                nc.scalar.activation(vrow[0:nk, r, :], aux[0:nk, r // 4, (r % 4) * P:(r % 4 + 1) * P],
                                                     ACT.Copy).then_inc(vwin_copied, 1)
                            nc.scalar.activation(krow[0:CHUNK + SAMPLE, 0, :], aux[0:CHUNK + SAMPLE, 1, P:2 * P],
                                                 ACT.Copy).then_inc(vwin_copied, 1)
                        else:
                            act.wait_ge(small_out, 4 * 16)
                            nc.scalar.activation(vrow[:, 0:4, :], aux[:, 0, :].rearrange("p (r n) -> p r n", r=4),
                                                 ACT.Copy).then_inc(vwin_copied, 1)
                            nc.scalar.activation(vrow[:, 4:7, :], aux[:, 1, 0:3 * P].rearrange("p (r n) -> p r n", r=3),
                                                 ACT.Copy).then_inc(vwin_copied, 1)
                            if blk.last:
                                nc.scalar.activation(krow[:, 1, :], aux[:, 1, 3 * P:4 * P], ACT.Copy).then_inc(vwin_copied, 1)
                    if u == 12:
                        for h in range(2):
                            act.wait_ge(mixed, blk.before(2) + h + 1)
                            nc.scalar.activation(mix_hi[:, 4 + 2 * h:6 + 2 * h, 0:n], tiles(rt, n)[:, 2 * h:2 * h + 2, :],
                                                 ACT.Copy).then_inc(lru_hi, 1)
                exps(blk, 0)
                for r in range(rounds):
                    if r + 1 < rounds:
                        exps(blk, r + 1)
                    if r % 2 == 1:
                        step1(blk, Z1 + r // 2)
                    if r:
                        attn_high(blk, r - 1)
                    copy_pT(blk, r)
                for h in range(rounds, 8):
                    if h % 2 == 1:
                        step1(blk, Z1 + h // 2)
                    if h == rounds:
                        attn_high(blk, rounds - 1)
                if blk.last:
                    act.wait_ge(state_t, 1)
                    nc.scalar.activation(state_rows[:, :], aux[0:32, 0, 0:P], ACT.Copy).then_inc(state_copied, 1)
                    for h in range(4):
                        step1(blk, 18 + h)
                else:
                    act.wait_ge(freed, 2 + blk.before(USES) + Z1 + 8)
                    copy_x(nxt, 0)
                    copy_x(nxt, 1)
                    step1(blk, 18)
                    copy_x(nxt, 2)
                    copy_x(nxt, 3)
                    prepare_x(nxt, range(0, 3))
                    step1(blk, 19)
                    prepare_x(nxt, range(3, 6))
                    step1(blk, 20)
                    prepare_x(nxt, range(6, 8))
                    step1(blk, 21)

            first = Block1(0)
            act.wait_ge(vec_t, 1)
            nc.scalar.activation(vec[:, :], aux[:, 0, 0:VROWS], ACT.Copy).then_inc(vec_ready, 1)
            act.wait_ge(raw_in[0], 32)
            for n in range(2):
                nc.scalar.activation(like_unit1(w_hi[n], n), raw_unit1(n), ACT.Copy).then_inc(w_hi_done, 1)
            for r in range(3):
                copy_x(first, r)
            act.wait_ge(vec_ready, 1)
            prepare_x(first, range(KT))
            act.wait_ge(cache_t, 1)
            nc.scalar.activation(kT[:, K_SAMPLE:K_SAMPLE + CHUNK], aux[:, 1, 0:CHUNK], ACT.Copy).then_inc(cache_copied, 1)
            nc.scalar.activation(vT[:, K_SAMPLE:K_SAMPLE + CHUNK], aux[:, 1, CHUNK:2 * CHUNK], ACT.Copy).then_inc(cache_copied, 1)
            act.wait_ge(setup_done, 1)
            nc.scalar.activation(tiny[:, 2, :], tiny[:, 1, :], ACT.Exp, scale=-1.0).then_inc(decay_e, 1)
            act.wait_ge(setup_done, 2)
            mix_block(first)
            with act.Fori(1, NB1) as b:
                chain.enter(b - 1, LT)
                mix_block(Block1(b))
            chain.leave(NB1 - 1)
            mix_block(Block1(NB1, last=True))

            def step2(b, n, more=True):
                act.wait_ge(unit_done, b * U2 + n + 1)
                if n + 2 < U2 or more:
                    split2(b, n + 2)

            def deviation2(b):
                act.wait_ge(sum2_all, b + 1)
                nc.scalar.activation(rstd2[:, :], aux[:, 0, 0:B2], ACT.Sqrt, scale=1.0 / D, bias=eps_t[:, 0:1]).then_inc(std2_done, 1)

            def hn_high(b, c):
                act.wait_ge(hn_done, 8 * b + c + 1)
                nc.scalar.activation(hn_hi[:, c, :], hn_t[:, :], ACT.Copy).then_inc(hn_hi_done, 1)

            def y_deviation(b, r):
                act.wait_ge(yT_ready, 4 * b + r + 1)
                act.wait_ge(y_stored, 16 * (4 * b + r) + 16)
                nc.scalar.activation(yout[0:YR, :], aux[0:YR, :, :], ACT.Square, accum_out=ystat[0:YR, 0:1]).then_inc(act_chain, 1)
                chain.n += 1
                act.wait_ge(act_chain, chain.base + chain.n)
                nc.scalar.activation(ystat[0:YR, 1:2], ystat[0:YR, 0:1], ACT.Sqrt, scale=1.0 / D, bias=eps_t[0:YR, 0:1])\
                  .then_inc(ystd_done, 1)

            def up(b, flush):
                for j in range(FT):
                    act.wait_ge(unit_done, b * U2 + j + 1)
                    if j >= 2:
                        act.wait_ge(hid_lo_done, 32 * b + j - 1)
                    nc.scalar.activation(act_t[:, j % 2, :], banks[j % 2][:, 0:B2], ACT.Relu).then_inc(relu_done, 1)
                    split2(b, j + 2)
                    act.wait_ge(relu_done, 32 * b + j + 1)
                    nc.scalar.activation(act_t[:, j % 2, :], act_t[:, j % 2, :], ACT.Square).then_inc(sq_done, 1)
                    if flush and j in (2, 4, 6, 8):
                        y_deviation(b - 1, j // 2 - 1)

            def down(b, prepare, more=True):
                for m in range(32):
                    step2(b, 32 + m, more)
                    if prepare and m == 4:
                        deviation2(b + 1)
                    if prepare and m >= 7 and (m - 7) % 3 == 0 and (m - 7) // 3 < KT:
                        hn_high(b + 1, (m - 7) // 3)

            deviation2(0)
            for c in range(KT):
                hn_high(0, c)
            up(0, False)
            with act.Fori(0, NB2 - 1) as b:
                chain.enter(b, 4)
                down(b, True)
                up(b + 1, True)
            chain.leave(NB2 - 1)
            down(NB2 - 1, False, more=False)
            for r in range(4):
                y_deviation(NB2 - 1, r)

        @block.vector
        def _(dve):
            chain = Chain(dve, dve_chain)
            link = chain.link

            def split1(blk, n):
                dve.wait_ge(w_hi_done, blk.before(U1) + n + 1)
                m = n % U1
                nc.vector.tensor_tensor(like_unit1(w_lo[n % 2], m), raw_unit1(m), like_unit1(w_hi[n % 2].bitcast(F32), m),
                                        ALU.subtract).then_inc(w_lo_done, 1)

            def split2(b, n):
                dve.wait_ge(w_hi_done, G1 + b * U2 + n + 1)
                nc.vector.tensor_tensor(like_unit2(w_lo[n % 2]), raw_unit2(n % U2), like_unit2(w_hi[n % 2].bitcast(F32)),
                                        ALU.subtract).then_inc(w_lo_done, 1)

            def next_split(blk, n):
                if n + 2 >= U1 and blk.last:
                    split2(0, n + 2 - U1)
                else:
                    split1(blk, n + 2)

            def low_x(blk, cs):
                n = blk.n
                for c in cs:
                    dve.wait_ge(xg_hi_done, blk.before(8) + c + 1)
                    nc.vector.scalar_tensor_tensor(xg_lo[:, c, 0:n], xT[:, c, 0:n], vec[:, V_GMIX + c:V_GMIX + c + 1],
                                                   xg_hi.bitcast(F32)[:, c, 0:n], ALU.mult, ALU.subtract)\
                      .then_inc(xg_lo_done, 1)

            def take_z(blk, u):
                n, uses = blk.n, blk.before(USES)
                dve.wait_ge(ready, uses + u + 1)
                z = banks[u % 2]
                if u < LT:
                    parts = [(uT[:, u, a + 3:a + 3 + m], o, m) for a, o, m in blk.segs]
                elif u < 2 * LT:
                    parts = [(tiles(gT, n)[:, u - LT, :], 0, n)]
                elif u < 10:
                    t = (kT, vT)[u - 8]
                    if blk.first:
                        parts = [(t[:, CHUNK:CHUNK + FIRST], 0, FIRST),
                                 (t[:, K_SAMPLE + CHUNK:K_SAMPLE + CHUNK + SAMPLE], FIRST, SAMPLE)]
                    else:
                        parts = [(t[:, CHUNK:CHUNK + B1], 0, B1)]
                else:
                    j, hh = (u - 10) // 2, u % 2
                    m = FIRST if blk.first else B1
                    chunks = qT[:, j, 0:2 * m].rearrange("p (c h q) -> p c h q", h=2, q=CHUNK)[:, :, hh, :]
                    parts = [(chunks, 0, m)]
                    if blk.first:
                        parts.append((qT[:, j, 2 * m + hh * SAMPLE:2 * m + (hh + 1) * SAMPLE], m, SAMPLE))
                for k, (dst, o, m) in enumerate(parts):
                    a, b = z[:, o:o + m], rstd[:, o:o + m]
                    if len(dst.shape) == 3:
                        a, b = (x.rearrange("p (c q) -> p c q", q=CHUNK) for x in (a, b))
                    ins = nc.vector.tensor_tensor(dst, a, b, ALU.mult)
                    if k == len(parts) - 1:
                        ins.then_inc(freed, 1)

            def convolve(blk, j):
                n = blk.n
                dve.wait_ge(tap0, blk.before(4, 8) + len(blk.segs) * (j + 1))
                for t in range(1, TAPS):
                    for k, (a, o, m) in enumerate(blk.segs):
                        x = tiles(xc, n)[:, j, o:o + m]
                        ins = nc.vector.scalar_tensor_tensor(x, uT[:, j, a + t:a + t + m], vec[:, V_CW + 4 * t + j:V_CW + 4 * t + j + 1],
                                                             x, ALU.mult, ALU.add)
                        if k < len(blk.segs) - 1:
                            continue
                        if t < TAPS - 1:
                            link(ins)
                        else:
                            ins.then_inc(conv_done, 1)

            def bound(blk, r):
                _, qn, _, nk = blk.rounds[r]
                s, m = r % 2, slice(0, 2 * qn)
                sk, minus = (sink_s[m, t, :] if qn == SAMPLE else sink[m, t, :] for t in range(2))
                dve.wait_ge(scores_ready, blk.before(7, 5) + r + 1)
                link(nc.vector.tensor_reduce(soft[m, s, 0, :], scores_of(r, m)[:, :, 0:nk], AX_X, ALU.max))
                link(nc.vector.scalar_tensor_tensor(soft[m, s, 1, :], soft[m, s, 0, :], -SCALE, minus, ALU.mult, ALU.min))
                nc.vector.tensor_tensor(soft[m, s, 4, :], sk, soft[m, s, 1, :], ALU.add).then_inc(bound_done, 1)

            def share(blk, r):
                _, qn, _, _ = blk.rounds[r]
                s, m = r % 2, slice(0, 2 * qn)
                dve.wait_ge(exp_done, blk.before(7, 5) + r + 1)
                link(nc.vector.tensor_tensor(soft[m, s, 2, :], soft[m, s, 2, :], soft[m, s, 4, :], ALU.add))
                nc.vector.reciprocal(soft[m, s, 3, :], soft[m, s, 2, :]).then_inc(share_done, 1)

            def attn_low(blk, r):
                q0, qn, _, _ = blk.rounds[r]
                dve.wait_ge(o_hi, blk.before(7, 5) + r + 1)
                nc.vector.tensor_tensor(mix_lo[:, 0:4, q0:q0 + qn], banks[5][:, 0:4 * qn].rearrange("p (t n) -> p t n", t=4),
                                        mix_hi.bitcast(F32)[:, 0:4, q0:q0 + qn], ALU.subtract).then_inc(o_lo, 1)

            def take_out(blk, h):
                n, u, d = blk.n, Z1 + h, h % 8
                dve.wait_ge(ready, blk.before(USES) + u + 1)
                if h == 0 and not blk.first:
                    dve.wait_ge(h_stored, blk.before(32, 64))
                if h == 8:
                    dve.wait_ge(freed, 2 + blk.before(USES) + Z1 + 8)
                other = xT if h < 8 else hacc
                nc.vector.tensor_tensor(hacc[:, d, 0:n], banks[u % 2][:, 0:n], other[:, d, 0:n], ALU.add).then_inc(freed, 1)

            def mix_block(blk):
                n, rounds = blk.n, len(blk.rounds)
                nxt = blk.next()
                end = FIRST if blk.first else B1
                dve.wait_ge(std_done, blk.before(1) + 1)
                link(nc.vector.reciprocal(rstd[:, 0:n], rstd[:, 0:n]))
                for u in range(Z1):
                    take_z(blk, u)
                    next_split(blk, u)
                    if u < LT:
                        convolve(blk, u)
                    if u == LT:
                        dve.wait_ge(conv_done, blk.before(4) + 4)
                        if blk.first:
                            link(nc.vector.tensor_copy(state[:, 12:24].rearrange("p (t j) -> p j t", t=3),
                                                       uT[:, :, FIRST + SAMPLE + 3:FIRST + SAMPLE + 6]))
                        if blk.last:
                            link(nc.vector.tensor_copy(state[:, 0:12].rearrange("p (t j) -> p j t", t=3), uT[:, :, B1:B1 + 3]))
                        link(nc.vector.tensor_copy(uT[:, :, 0:3], uT[:, :, end:end + 3]))
                    if u in (7, 8):
                        h = u - 7
                        q0, t, m = (pair(x, n, h) for x in (av, rt, xc))
                        dve.wait_ge(tanh_done, blk.before(4) + 2 * h + 2)
                        link(nc.vector.tensor_scalar(q0, q0, 0.5, 0.5, ALU.mult, ALU.add))
                        dve.wait_ge(ix_done, blk.before(2) + h + 1)
                        nc.vector.scalar_tensor_tensor(m, t, 1.0, q0, ALU.add, ALU.mult).then_inc(newton, 1)
                        dve.wait_ge(newton, blk.before(2) + h + 1)
                        link(nc.vector.scalar_tensor_tensor(q0, m, 2.0, q0, ALU.subtract, ALU.mult))
                    if u in (9, 10):
                        h = u - 9
                        dve.wait_ge(sqrt_done, blk.before(2) + h + 1)
                        nc.vector.scalar_tensor_tensor(pair(rt, n, h), pair(av, n, h), -1.0, pair(rt, n, h), ALU.mult, ALU.mult)\
                          .then_inc(drive, 1)
                        dve.wait_ge(drive, blk.before(2) + h + 1)
                        link(nc.vector.tensor_scalar(pair(av, n, h), pair(av, n, h), -2.0, -1.0, ALU.mult, ALU.add))
                    if u == 11:
                        for j in range(LT):
                            if j % 2 == 0:
                                dve.wait_ge(scan_in, blk.before(2) + j // 2 + 1)
                            for s, (_, o, m) in enumerate(blk.segs):
                                if not blk.first:
                                    start = carry[:, j:j + 1]
                                else:
                                    start = vec[:, V_SL + j:V_SL + j + 1] if s else 0.0
                                x = tiles(xc, n)[:, j, o:o + m]
                                ins = nc.vector.tensor_tensor_scan(x, tiles(av, n)[:, j, o:o + m], tiles(ix, n)[:, j, o:o + m],
                                                                   start, ALU.mult, ALU.add)
                        link(ins)
                    if u == 12:
                        dve.wait_ge(gelu_done, blk.before(1) + 1)
                        for h in range(2):
                            nc.vector.tensor_tensor(pair(rt, n, h), pair(gT, n, h), pair(xc, n, h), ALU.mult).then_inc(mixed, 1)
                        link(nc.vector.tensor_copy(carry[:, :].rearrange("p (j o) -> p j o", o=1), tiles(xc, n)[:, :, end - 1:end]))
                        if blk.first:
                            link(nc.vector.tensor_copy(state[:, 28:32].rearrange("p (j o) -> p j o", o=1), tiles(xc, n)[:, :, n - 1:n]))
                        if blk.last:
                            nc.vector.tensor_copy(state[:, 24:28], carry[:, :]).then_inc(state_set, 1)
                for h in range(2):
                    dve.wait_ge(lru_hi, blk.before(2) + h + 1)
                    nc.vector.tensor_tensor(mix_lo[:, 4 + 2 * h:6 + 2 * h, 0:n], tiles(rt, n)[:, 2 * h:2 * h + 2, :],
                                            mix_hi.bitcast(F32)[:, 4 + 2 * h:6 + 2 * h, 0:n], ALU.subtract).then_inc(lru_lo, 1)
                bound(blk, 0)
                for r in range(rounds):
                    if r + 1 < rounds:
                        bound(blk, r + 1)
                    share(blk, r)
                    take_out(blk, r)
                    if r % 2 == 1:
                        next_split(blk, Z1 + r // 2)
                    if r:
                        attn_low(blk, r - 1)
                link(nc.vector.tensor_copy(kT[:, 0:CHUNK], kT[:, end:end + CHUNK]))
                nc.vector.tensor_copy(vT[:, 0:CHUNK], vT[:, end:end + CHUNK]).then_inc(halo_done, 1)
                for h in range(rounds, 8):
                    take_out(blk, h)
                    if h % 2 == 1:
                        next_split(blk, Z1 + h // 2)
                    if h == rounds:
                        attn_low(blk, rounds - 1)
                for couple in range(4):
                    take_out(blk, 8 + 2 * couple)
                    take_out(blk, 9 + 2 * couple)
                    next_split(blk, 18 + couple)
                    if nxt and couple >= 1:
                        low_x(nxt, range(3 * (couple - 1), min(3 * couple, KT)))

            nc.vector.memset(eps_t[:, :], EPS).then_inc(freed, 2)
            link(nc.vector.memset(uT[:, :, 0:3], 0.0))
            link(nc.vector.memset(soft[:, :, :, :], 0.0))
            dve.wait_ge(const_in, 14 * 16)
            for hh in range(2):
                s8 = sink8[:, :].rearrange("p (a h) -> p a h", h=2)
                for t, sign in enumerate((1.0, -1.0)):
                    nc.vector.tensor_scalar(sink[hh * HEAD:(hh + 1) * HEAD, t, :], s8[hh * HEAD:(hh + 1) * HEAD, :, hh],
                                            sign, None, ALU.mult)
                    nc.vector.tensor_scalar(sink_s[hh * SAMPLE:(hh + 1) * SAMPLE, t, :],
                                            s8[hh * SAMPLE:(hh + 1) * SAMPLE, :, hh], sign, None, ALU.mult)
            dve.wait_ge(vec_ready, 1)
            link(nc.vector.tensor_copy(uT[:, :, FIRST + 3:FIRST + 6], vec[:, V_SC:V_SC + 12].rearrange("p (t j) -> p j t", t=3)))
            lam = vec[:, V_LAM:V_LAM + LT]
            neg, mag, e, s1, s2, ser, pos = (tiny[:, k, :] for k in range(7))
            link(nc.vector.tensor_scalar(neg, lam, -1.0, None, ALU.mult))
            nc.vector.tensor_tensor(mag, lam, neg, ALU.max).then_inc(setup_done, 1)
            dve.wait_ge(decay_e, 1)
            link(nc.vector.tensor_scalar(s1, e, 2.0, None, ALU.add))
            link(nc.vector.reciprocal(s1, s1))
            link(nc.vector.tensor_tensor(s1, s1, e, ALU.mult))
            link(nc.vector.tensor_tensor(s2, s1, s1, ALU.mult))
            link(nc.vector.tensor_scalar(ser, s2, 1.0 / 17, 1.0 / 15, ALU.mult, ALU.add))
            for k in (13, 11, 9, 7, 5, 3, 1):
                link(nc.vector.tensor_tensor(ser, ser, s2, ALU.mult))
                link(nc.vector.tensor_scalar(ser, ser, 1.0 / k, None, ALU.add))
            link(nc.vector.tensor_tensor(ser, ser, s1, ALU.mult))
            link(nc.vector.tensor_scalar(pos, neg, 0.0, None, ALU.max))
            link(nc.vector.scalar_tensor_tensor(pos, ser, 2.0, pos, ALU.mult, ALU.add))
            nc.vector.tensor_scalar(decay[:, 0, :], pos, -8.0, None, ALU.mult)
            nc.vector.tensor_scalar(decay[:, 1, :], pos, 4.0, None, ALU.mult).then_inc(setup_done, 1)
            dve.wait_ge(setup_done, 2)

            first = Block1(0)
            split1(first, 0)
            split1(first, 1)
            low_x(first, range(KT))
            mix_block(first)
            with dve.Fori(1, NB1) as b:
                chain.enter(b - 1, CHAIN1)
                mix_block(Block1(b))
            chain.leave(NB1 - 1)
            mix_block(Block1(NB1, last=True))

            def deviation2(b):
                dve.wait_ge(std2_done, b + 1)
                link(nc.vector.reciprocal(rstd2[:, :], rstd2[:, :]))

            def normalise2(b, c):
                if c:
                    dve.wait_ge(hn_lo_done, 8 * b + c)
                nc.vector.scalar_tensor_tensor(hn_t[:, :], hnext[:, c, :], vec[:, V_GFFN + c:V_GFFN + c + 1], rstd2[:, :],
                                               ALU.mult, ALU.mult).then_inc(hn_done, 1)
                dve.wait_ge(hn_hi_done, 8 * b + c + 1)
                nc.vector.tensor_tensor(hn_lo[:, c, :], hn_t[:, :], hn_hi.bitcast(F32)[:, c, :], ALU.subtract).then_inc(hn_lo_done, 1)

            def write_y(b, r):
                dve.wait_ge(ystd_done, 4 * b + r + 1)
                link(nc.vector.reciprocal(ystat[0:YR, 2:3], ystat[0:YR, 1:2]))
                nc.vector.scalar_tensor_tensor(yout[0:YR, :].rearrange("p (a n) -> p a n", a=2), aux[0:YR, :, :],
                                               ystat[0:YR, 2:3], gfin[0:YR, :].rearrange("p (a n) -> p a n", a=2),
                                               ALU.mult, ALU.mult).then_inc(yout_done, 1)

            def up(b, flush):
                for j in range(FT):
                    split2(b, j + 2)
                    dve.wait_ge(sq_done, 32 * b + j + 1)
                    nc.vector.tensor_copy(hid_hi[:, j, :], act_t[:, j % 2, :]).then_inc(hid_hi_done, 1)
                    dve.wait_ge(hid_hi_done, 32 * b + j + 1)
                    nc.vector.tensor_tensor(hid_lo[:, j, :], act_t[:, j % 2, :], hid_hi.bitcast(F32)[:, j, :], ALU.subtract)\
                      .then_inc(hid_lo_done, 1)
                    if flush and j in (2, 4, 6, 8):
                        write_y(b - 1, j // 2 - 1)

            def down(b, prepare, more=True):
                dve.wait_ge(hcur_in, 16 * b + 16)
                for m in range(32):
                    if m + 34 < U2 or more:
                        split2(b, m + 34)
                    if (m % 8) // 2 == 3:
                        d = 2 * (m // 8) + m % 2
                        dve.wait_ge(unit_done, b * U2 + 32 + m + 1)
                        nc.vector.tensor_tensor(hcur[:, d, :], banks[2 + (d // 2) % 2 * 2 + d % 2][:, 0:B2], hcur[:, d, :], ALU.add)\
                          .then_inc(y_done, 1)
                    if prepare and m == 4:
                        deviation2(b + 1)
                    if prepare and m >= 7 and (m - 7) % 3 == 0 and (m - 7) // 3 < KT:
                        normalise2(b + 1, (m - 7) // 3)

            dve.wait_ge(hnext_in, 16)
            nc.vector.memset(ystat[:, :], 0.0).then_inc(yout_done, 1)
            deviation2(0)
            for c in range(KT):
                normalise2(0, c)
            up(0, False)
            with dve.Fori(0, NB2 - 1) as b:
                chain.enter(b, 5)
                down(b, True)
                up(b + 1, True)
            chain.leave(NB2 - 1)
            down(NB2 - 1, False, more=False)
            for r in range(4):
                write_y(NB2 - 1, r)

        @block.tensor
        def _(pe):
            def product(out, w, wcols, hi, lo, ks, start=True, stop=True):
                for i, (kw, kx) in enumerate(ks):
                    for part, (a, x) in enumerate(((w_hi, hi), (w_hi, lo), (w_lo, hi))):
                        wt = a[w][:, kw * wcols[0] + wcols[1]:kw * wcols[0] + wcols[1] + P]
                        last = nc.tensor.matmul(out, wt, x(kx), start=(start and i == 0 and part == 0),
                                                stop=(stop and i == len(ks) - 1 and part == 2))
                return last

            def transpose_x(blk, r):
                if blk.first and r == 0:
                    pe.wait_ge(const_set, 4)
                pe.wait_ge(x_in[r % 2], 32 * (blk.before(2, 2 - r % 2) + r // 2 + 1))
                for half in range(2):
                    if r:
                        pe.wait_ge(xt_copied, blk.before(8, 6) + 2 * (r - 1) + half + 1)
                    elif not blk.first:
                        pe.wait_ge(vwin_copied, 6 + (blk.b - 1) * 2)
                    for c in range(4):
                        last = nc.tensor.transpose(aux[:, half, c * blk.xr:(c + 1) * blk.xr],
                                                   xrow[0:blk.xr, r % 2, (4 * half + c) * P:(4 * half + c + 1) * P],
                                                   ident[0:blk.xr, 0:blk.xr])
                    last.then_inc(xt_ready, 1)

            def scores(blk, r):
                q0, qn, k0, nk = blk.rounds[r]
                if r >= 2:
                    pe.wait_ge(exp_done, blk.before(7, 5) + r - 1)
                for a in range(4):
                    kv, j = a // 2, a % 2
                    m = slice(kv * HEAD, (kv + 1) * HEAD)
                    last = nc.tensor.matmul(scores_of(r, slice(0, 2 * qn))[:, a, 0:nk], qT[m, j, 2 * q0:2 * (q0 + qn)],
                                            kT[m, k0:k0 + nk], start=True, stop=True)
                last.then_inc(scores_ready, 1)

            def transpose_p(blk, r):
                _, qn, _, nk = blk.rounds[r]
                pe.wait_ge(probs_done, blk.before(7, 5) + r + 1)
                if r:
                    pe.wait_ge(pT_copied, blk.before(7, 5) + r)
                for a in range(4):
                    last = nc.tensor.transpose(banks[4][0:nk, a * P:a * P + 2 * qn], prob[0:2 * qn, r % 2, a, 0:nk],
                                               ident[0:2 * qn, 0:2 * qn])
                last.then_inc(pT_ready, 1)

            def attend(blk, r):
                _, qn, _, nk = blk.rounds[r]
                pe.wait_ge(pT_copied, blk.before(7, 5) + r + 1)
                if r:
                    pe.wait_ge(o_lo, blk.before(7, 5) + r)
                for kv in range(2):
                    m = slice(kv * HEAD, (kv + 1) * HEAD)
                    last = nc.tensor.matmul(banks[5][m, 0:4 * qn], vrow[0:nk, r, m], pT[0:nk, r % 2, 2 * kv:2 * kv + 2, 0:2 * qn],
                                            start=True, stop=True)
                last.then_inc(o_ready, 1)

            def out_half(blk, h):
                n, u, unit = blk.n, Z1 + h, Z1 + h // 2
                if h % 2 == 0:
                    pe.wait_ge(w_lo_done, blk.before(U1) + unit + 1)
                pe.wait_ge(freed, blk.before(USES) + u + 1)
                if h == 0:
                    pe.wait_ge(lru_lo, blk.before(2) + 2)
                if h == 8:
                    pe.wait_ge(o_lo, blk.before(7, 5) + len(blk.rounds))
                k0 = 4 if h < 8 else 0
                product(banks[u % 2][:, 0:n], unit % 2, (256, (h % 2) * P), lambda k: mix_hi[:, k, 0:n],
                        lambda k: mix_lo[:, k, 0:n], [(k, k0 + k) for k in range(4)]).then_inc(ready, 1)

            def mix_block(blk):
                n = blk.n
                uses, units = blk.before(USES), blk.before(U1)
                nxt = blk.next()
                pe.wait_ge(sum_done, blk.before(7) + 7)
                nc.tensor.matmul(aux[:, 0, 0:n], ones[:, :], sumsq[:, 0:n], start=True, stop=True).then_inc(sum_all, 1)
                for u in range(Z1):
                    pe.wait_ge(w_lo_done, units + u + 1)
                    pe.wait_ge(freed, uses + u + 1)
                    if u == 0:
                        for c in range(KT):
                            pe.wait_ge(xg_lo_done, blk.before(8) + c + 1)
                            last = product(banks[0][:, 0:n], 0, (P, 0), lambda k: xg_hi[:, k, 0:n],
                                           lambda k: xg_lo[:, k, 0:n], [(c, c)], start=c == 0, stop=c == KT - 1)
                    else:
                        last = product(banks[u % 2][:, 0:n], u % 2, (P, 0), lambda k: xg_hi[:, k, 0:n],
                                       lambda k: xg_lo[:, k, 0:n], [(c, c) for c in range(KT)])
                    last.then_inc(ready, 1)
                    if 2 <= u < 6:
                        j = u - 2
                        pe.wait_ge(conv_done, blk.before(4) + j + 1)
                        for g in range(2):
                            if j:
                                pe.wait_ge(sig_done, blk.before(8) + 2 * j - 1 + g)
                            elif g == 0:
                                pe.wait_ge(std_done, blk.before(1) + 1)
                            nc.tensor.matmul(aux[:, g, 0:n], gate_w[:, g, j, :], tiles(xc, n)[:, j, :], start=True, stop=True)\
                              .then_inc(gates_ready, 1)
                    if u == 10:
                        pe.wait_ge(freed, 2 + uses + 10)
                        pe.wait_ge(sig_done, blk.before(8) + 8)
                        if not blk.first:
                            pe.wait_ge(halo_done, blk.before(1))
                        for g in range(2):
                            for r, (_, _, k0, nk) in list(enumerate(blk.rounds))[4 * g:4 * g + 4]:
                                last = nc.tensor.transpose(aux[0:nk, g, (r % 4) * P:(r % 4 + 1) * P], vT[:, k0:k0 + nk], ident[:, :])
                            if g == 1 and blk.first:
                                last = nc.tensor.transpose(aux[0:CHUNK + SAMPLE, 1, P:2 * P],
                                                           kT[:, K_SAMPLE:K_SAMPLE + CHUNK + SAMPLE], ident[:, :])
                            if g == 1 and blk.last:
                                last = nc.tensor.transpose(aux[:, 1, 3 * P:4 * P], kT[:, B1 - CHUNK:B1 + CHUNK], ident[:, :])
                            last.then_inc(vwin_ready, 1)
                pe.wait_ge(freed, 2 + uses + Z1)
                pe.wait_ge(vwin_copied, 6 if blk.first else 6 + (blk.b - 1) * 2 + 2 + blk.last)
                scores(blk, 0)
                scores(blk, 1)
                for r in range(len(blk.rounds)):
                    out_half(blk, r)
                    if r:
                        attend(blk, r - 1)
                    transpose_p(blk, r)
                    if r + 2 < len(blk.rounds):
                        scores(blk, r + 2)
                for h in range(len(blk.rounds), 8):
                    out_half(blk, h)
                    if h == len(blk.rounds):
                        attend(blk, h - 1)
                if blk.last:
                    pe.wait_ge(state_set, 1)
                    pe.wait_ge(vwin_copied, 6 + NB1 * 2 + 1)
                    nc.tensor.transpose(aux[0:32, 0, 0:P], state[:, :], ident[:, :]).then_inc(state_t, 1)
                    for h in range(8, 16):
                        out_half(blk, h)
                else:
                    transpose_x(nxt, 0)
                    transpose_x(nxt, 1)
                    out_half(blk, 8)
                    out_half(blk, 9)
                    transpose_x(nxt, 2)
                    transpose_x(nxt, 3)
                    for h in range(10, 16):
                        out_half(blk, h)

            first = Block1(0)
            pe.wait_ge(const_set, 4)
            pe.wait_ge(const_in, 14 * 16)
            nc.tensor.transpose(aux[:, 0, 0:VROWS], vrows[:, :], ident[0:VROWS, 0:VROWS]).then_inc(vec_t, 1)
            pe.wait_ge(vec_ready, 1)
            for r in range(3):
                transpose_x(first, r)
            pe.wait_ge(cache_in, 32)
            pe.wait_ge(xt_copied, 6)
            nc.tensor.transpose(aux[:, 1, 0:CHUNK], cache_rows[:, 0, :], ident[0:CHUNK, 0:CHUNK])
            nc.tensor.transpose(aux[:, 1, CHUNK:2 * CHUNK], cache_rows[:, 1, :], ident[0:CHUNK, 0:CHUNK]).then_inc(cache_t, 1)
            pe.wait_ge(cache_copied, 2)
            mix_block(first)
            with pe.Fori(1, NB1) as b:
                mix_block(Block1(b))
            mix_block(Block1(NB1, last=True))

            def sum_all2(b):
                pe.wait_ge(sum2_done, 7 * b + 7)
                nc.tensor.matmul(aux[:, 0, 0:B2], ones[:, :], sumsq2[:, :], start=True, stop=True).then_inc(sum2_all, 1)

            def transpose_y(b, r):
                if r:
                    pe.wait_ge(yout_done, 1 + 4 * b + r)
                for c in range(KT):
                    last = nc.tensor.transpose(aux[0:YR, c // 4, (c % 4) * P:(c % 4 + 1) * P], hcur[:, c, r * YR:(r + 1) * YR],
                                               ident[:, :])
                last.then_inc(yT_ready, 1)

            def up(b, flush):
                for j in range(FT):
                    pe.wait_ge(w_lo_done, G1 + b * U2 + j + 1)
                    if j >= 2:
                        pe.wait_ge(relu_done, 32 * b + j - 1)
                    if j == 0:
                        for c in range(KT):
                            pe.wait_ge(hn_lo_done, 8 * b + c + 1)
                            last = product(banks[0][:, 0:B2], 0, (P, 0), lambda k: hn_hi[:, k, :], lambda k: hn_lo[:, k, :],
                                           [(c, c)], start=c == 0, stop=c == KT - 1)
                    else:
                        last = product(banks[j % 2][:, 0:B2], j % 2, (P, 0), lambda k: hn_hi[:, k, :], lambda k: hn_lo[:, k, :],
                                       [(c, c) for c in range(KT)])
                    last.then_inc(unit_done, 1)
                    if flush and j in (1, 3, 5, 7):
                        if j == 1:
                            pe.wait_ge(y_done, 8 * b)
                            pe.wait_ge(std2_done, b + 1)
                        transpose_y(b - 1, j // 2)

            def down(b, prepare):
                for m in range(32):
                    dp, kq, a = m // 8, (m % 8) // 2, m % 2
                    pe.wait_ge(w_lo_done, G1 + b * U2 + 32 + m + 1)
                    if dp == 0 and a == 0:
                        pe.wait_ge(hid_lo_done, 32 * b + 8 * (kq + 1))
                    if dp >= 2 and kq == 0:
                        pe.wait_ge(y_done, 8 * b + 2 * (dp - 2) + a + 1)
                    product(banks[2 + dp % 2 * 2 + a][:, 0:B2], m % 2, (P, 0), lambda k: hid_hi[:, k, :],
                            lambda k: hid_lo[:, k, :], [(c, kq * KT + c) for c in range(KT)],
                            start=kq == 0, stop=kq == 3).then_inc(unit_done, 1)
                    if prepare and m == 3:
                        pe.wait_ge(yout_done, 1 + 4 * b)
                        sum_all2(b + 1)

            sum_all2(0)
            up(0, False)
            with pe.Fori(0, NB2 - 1) as b:
                down(b, True)
                up(b + 1, True)
            down(NB2 - 1, False)
            pe.wait_ge(y_done, 8 * NB2)
            for r in range(4):
                transpose_y(NB2 - 1, r)


_INS = ['x_prompt', 'x_sample', 'cache_k', 'cache_v', 'state_conv', 'state_lru', 'norm_mix_g', 'w_in', 'attn_sinks',
        'conv_w', 'conv_b', 'gate_a_w', 'gate_a_b', 'gate_x_w', 'gate_x_b', 'lru_lambda', 'w_out', 'norm_ffn_g',
        'w_up', 'w_down', 'final_norm_g']
_OUTS = [(1, SEQ, D), (1, SAMPLE, D), (1, 1, WINDOW, 2, HEAD), (1, 1, WINDOW, 2, HEAD), (1, 1, TAPS - 1, LRU), (1, 1, LRU),
         (1, 1, WINDOW, 2, HEAD), (1, 1, WINDOW, 2, HEAD), (1, 1, TAPS - 1, LRU), (1, 1, LRU)]


def kernel(**inputs):
    import concourse.bacc as bacc
    from concourse.bass_utils import run_bass_kernel_spmd

    nc = bacc.Bacc("TRN2", target_bir_lowering=False, num_devices=1)
    arrays, args = {}, []
    for name in _INS:
        a = np.ascontiguousarray(inputs[name])
        arrays[f"in_{name}"] = a
        args.append(nc.dram_tensor(f"in_{name}", a.shape, mybir.dt.from_np(a.dtype), kind="ExternalInput").ap())
    for i, shape in enumerate(_OUTS):
        args.append(nc.dram_tensor(f"out_{i}", shape, F32, kind="ExternalOutput").ap())
    build_program(nc, *args)
    r = run_bass_kernel_spmd(nc, [arrays], core_ids=[0])
    return tuple(r.results[0][f"out_{i}"] for i in range(len(_OUTS)))
```

```python
from contextlib import ExitStack

import numpy as np
import concourse.bass as bass
from concourse import mybir

F32 = mybir.dt.float32
F32R = mybir.dt.float32r
ALU = mybir.AluOpType
ACT = mybir.ActivationFunctionType
AX_X = mybir.AxisListType.X

P = 128
D = 1024
SEQ = 2048
SAMPLE = 32
TOKENS = SEQ + SAMPLE
CHUNK = 64
WINDOW = 128
HEAD = 64
KT = D // P
FF = 4 * D
FT = FF // P
LT = 4
ATTN = 512
LRU = 512
TAPS = 4
SCALE = HEAD ** -0.5
EPS = 1e-6

B1 = 448
NB1 = 4
FIRST = SEQ - NB1 * B1
XR, XR0 = 112, 96
B2 = 416
NB2 = TOKENS // B2
YR = 104
Z1 = 14
U1 = Z1 + 8
USES = Z1 + 16
L1 = 6
U2 = 64
L2 = 16
G1 = U1 * (NB1 + 1)
K_SAMPLE = CHUNK + FIRST

CHAIN1 = 41
V_GMIX, V_GFFN, V_CW, V_CB, V_BA, V_BX, V_LAM, V_SC, V_SL = 0, 8, 16, 32, 36, 40, 44, 48, 60
VROWS = 64


class Chain:

    def __init__(self, eng, sem):
        self.eng, self.sem, self.base, self.n = eng, sem, 0, 0

    def link(self, ins):
        ins.then_inc(self.sem, 1)
        self.n += 1
        self.eng.wait_ge(self.sem, self.base + self.n)

    def enter(self, i, stride):
        self.start, self.stride = self.n, stride
        self.base, self.n = self.start + i * stride, 0

    def leave(self, times):
        assert self.n == self.stride, (self.n, self.stride)
        self.base, self.n = 0, self.start + times * self.stride


class Block1:

    def __init__(self, b, last=False):
        self.b, self.last = b, last
        self.first = isinstance(b, int) and b == 0
        self.n = FIRST + SAMPLE if self.first else B1
        self.xr = XR0 if self.first else XR
        self.tiles = self.n // self.xr
        self.segs = [(0, 0, FIRST), (FIRST + 3, FIRST, SAMPLE)] if self.first else [(0, 0, B1)]
        if self.first:
            self.rounds = [(0, CHUNK, CHUNK, CHUNK)]
            self.rounds += [(CHUNK * c, CHUNK, CHUNK * c, WINDOW) for c in range(1, FIRST // CHUNK)]
            self.rounds += [(FIRST, SAMPLE, K_SAMPLE, CHUNK + SAMPLE)]
        else:
            self.rounds = [(CHUNK * c, CHUNK, CHUNK * c, WINDOW) for c in range(B1 // CHUNK)]

    def before(self, each, in_first=None):
        if self.first:
            return 0
        return (each if in_first is None else in_first) + (self.b - 1) * each

    def next(self):
        return None if self.last else Block1(self.b + 1)


def use_after(n):
    return n + 1 if n < Z1 else Z1 + 2 * (n - Z1 + 1)


def build_program(nc, x_prompt, x_sample, cache_k, cache_v, state_conv, state_lru, norm_mix_g, w_in, attn_sinks,
                  conv_w, conv_b, gate_a_w, gate_a_b, gate_x_w, gate_x_b, lru_lambda, w_out, norm_ffn_g, w_up,
                  w_down, final_norm_g, y_prompt, y_sample, nk_prompt, nv_prompt, nconv_prompt, nlru_prompt,
                  nk_sample, nv_sample, nconv_sample, nlru_sample):
    ctx = ExitStack()
    with ctx:
        h_dram = nc.dram_tensor("h_scratch", (P, KT, TOKENS), F32, kind="Internal").ap()

        def sb(name, shape, dt=F32):
            return ctx.enter_context(nc.sbuf_tensor(name, shape, dt))

        def sem(name):
            return ctx.enter_context(nc.semaphore(name))

        raw = sb("raw", [P, 2, 2 * D])
        w_hi = [sb(f"w_hi{s}", [P, D], F32R) for s in range(2)]
        w_lo = [sb(f"w_lo{s}", [P, D], F32R) for s in range(2)]
        ident = sb("ident", [P, P])
        ones = sb("ones", [P, P])
        vec = sb("vec", [P, VROWS])
        eps_t = sb("eps_t", [P, 1])

        phase1 = ExitStack()

        def sb1(name, shape, dt=F32):
            return phase1.enter_context(nc.sbuf_tensor(name, shape, dt))

        xg_hi = sb1("xg_hi", [P, KT, B1], F32R)
        xg_lo = sb1("xg_lo", [P, KT, B1], F32R)
        xrow = sb1("xrow", [P, 2, D])
        xc = sb1("xc", [P, LT * B1])
        av = sb1("av", [P, LT * B1])
        ix = sb1("ix", [P, LT * B1])
        gT = sb1("gT", [P, LT * B1])
        xT = sb1("xT", [P, KT, B1])
        hacc = sb1("hacc", [P, KT, B1])
        mix_hi = sb1("mix_hi", [P, KT, B1], F32R)
        mix_lo = sb1("mix_lo", [P, KT, B1], F32R)
        uT = sb1("uT", [P, LT, B1 + 3])
        kT = sb1("kT", [P, CHUNK + B1])
        vT = sb1("vT", [P, CHUNK + B1])
        qT = sb1("qT", [P, 2, 2 * B1])
        rt = sb1("rt", [P, LT * B1])
        carry = sb1("carry", [P, LT])
        vrow = sb1("vrow", [P, 7, P])
        prob = sb1("prob", [P, 2, 4, WINDOW])
        pT = sb1("pT", [P, 2, 4, P])
        sq = sb1("sq", [P, 2, B1])
        sumsq = sb1("sumsq", [P, B1])
        rstd = sb1("rstd", [P, B1])
        gate_w = sb1("gate_w", [P, 2, LT, P])
        sink8 = sb1("sink8", [P, 8])
        sink = sb1("sink", [P, 2, 4])
        sink_s = sb1("sink_s", [CHUNK, 2, 4])
        soft = sb1("soft", [P, 2, 5, 4])
        decay = sb1("decay", [P, 2, LT])
        tiny = sb1("tiny", [P, 8, LT])
        vrows = sb1("vrows", [VROWS, P])
        cache_rows = sb1("cache_rows", [CHUNK, 2, P])
        state = sb1("state", [P, 32])
        state_rows = sb1("state_rows", [32, P])
        krow = sb1("krow", [P, 2, P])
        phase1.close()

        phase2 = ExitStack()

        def sb2(name, shape, dt=F32):
            return phase2.enter_context(nc.sbuf_tensor(name, shape, dt))

        hnext = sb2("hnext", [P, KT, B2])
        hn_hi = sb2("hn_hi", [P, KT, B2], F32R)
        hn_t = sb2("hn_t", [P, B2])
        rstd2 = sb2("rstd2", [P, B2])
        sq2 = sb2("sq2", [P, B2])
        sumsq2 = sb2("sumsq2", [P, B2])
        hn_lo = sb2("hn_lo", [P, KT, B2], F32R)
        act_t = sb2("act_t", [P, 2, B2])
        hid_hi = sb2("hid_hi", [P, FT, B2], F32R)
        hid_lo = sb2("hid_lo", [P, FT, B2], F32R)
        hcur = sb2("hcur", [P, KT, B2])
        gfin = sb2("gfin", [P, D])
        yout = sb2("yout", [P, D])
        ystat = sb2("ystat", [P, 4, 3])
        phase2.close()

        scores_a = ctx.enter_context(nc.psum_tensor("scores_a", [P, 2, 512], F32))
        results = ctx.enter_context(nc.psum_tensor("results", [P, 2, 512], F32))
        last_banks = [ctx.enter_context(nc.psum_tensor(f"bank{b}", [P, 512], F32)) for b in (4, 5)]
        banks = [results[:, 0, :], results[:, 1, :], scores_a[:, 0, :], scores_a[:, 1, :]] + last_banks
        aux = ctx.enter_context(nc.psum_tensor("aux", [P, 2, 512], F32))

        raw_in = [sem(f"raw_in{s}") for s in range(2)]
        w_hi_done, w_lo_done = sem("w_hi_done"), sem("w_lo_done")
        const_in, vec_in, const_set, vec_ready = sem("const_in"), sem("vec_in"), sem("const_set"), sem("vec_ready")
        vec_t, decay_e, setup_done = sem("vec_t"), sem("decay_e"), sem("setup_done")
        x_in = [sem(f"x_in{r}") for r in range(4)]
        xt_ready, xt_copied, x_sq, sum_done = sem("xt_ready"), sem("xt_copied"), sem("x_sq"), sem("sum_done")
        xg_hi_done, xg_lo_done = sem("xg_hi_done"), sem("xg_lo_done")
        sum_all, std_done = sem("sum_all"), sem("std_done")
        ready, freed = sem("ready"), sem("freed")
        tap0, conv_done, gates_ready, sig_done = sem("tap0"), sem("conv_done"), sem("gates_ready"), sem("sig_done")
        ix_done, tanh_done, newton, sqrt_done = sem("ix_done"), sem("tanh_done"), sem("newton"), sem("sqrt_done")
        drive, scan_in, gelu_done, mixed = sem("drive"), sem("scan_in"), sem("gelu_done"), sem("mixed")
        lru_hi, lru_lo = sem("lru_hi"), sem("lru_lo")
        vwin_ready, vwin_copied = sem("vwin_ready"), sem("vwin_copied")
        scores_ready, bound_done, exp_done = sem("scores_ready"), sem("bound_done"), sem("exp_done")
        share_done = sem("share_done")
        probs_done, pT_ready, pT_copied = sem("probs_done"), sem("pT_ready"), sem("pT_copied")
        o_ready, o_hi, o_lo = sem("o_ready"), sem("o_hi"), sem("o_lo")
        h_stored = sem("h_stored")
        halo_done = sem("halo_done")
        cache_in, cache_t, cache_copied = sem("cache_in"), sem("cache_t"), sem("cache_copied")
        state_set, state_t, state_copied = sem("state_set"), sem("state_t"), sem("state_copied")
        small_out = sem("small_out")
        dve_chain, act_chain, pool_chain = sem("dve_chain"), sem("act_chain"), sem("pool_chain")
        hnext_in, hcur_in = sem("hnext_in"), sem("hcur_in")
        sum2_done, sum2_all, std2_done = sem("sum2_done"), sem("sum2_all"), sem("std2_done")
        hn_done, hn_hi_done, hn_lo_done = sem("hn_done"), sem("hn_hi_done"), sem("hn_lo_done")
        unit_done = sem("unit_done")
        relu_done, sq_done, hid_hi_done, hid_lo_done = sem("relu_done"), sem("sq_done"), sem("hid_hi_done"), sem("hid_lo_done")
        y_done, yT_ready, ystd_done, yout_done, y_stored = sem("y_done"), sem("yT_ready"), sem("ystd_done"), sem("yout_done"), sem("y_stored")

        block = ctx.enter_context(nc.Block())

        xp, xs = x_prompt[0], x_sample[0]
        win_v = w_in[0].rearrange("(c p) n -> p c n", p=P)
        wout_lru = w_out[0, ATTN:ATTN + LRU, :].rearrange("(c p) n -> p c n", p=P)
        wout_attn = [w_out[0, kv * 256:(kv + 1) * 256, :].rearrange("(t d) n -> d t n", d=HEAD) for kv in range(2)]
        wup_v = w_up[0].rearrange("(c p) n -> p c n", p=P)
        wdown_v = w_down[0].rearrange("(k c p) n -> k p c n", p=P, c=KT)
        UNIT_COLS = [768, 1024, 1280, 1536, 512]

        def load_of1(n):
            return n // 2 if n < 20 else n - 10

        def raw_unit1(n):
            r, a = raw[:, load_of1(n) % 2, :], n % 2
            if n < 10:
                return r.rearrange("p (c n) -> p c n", c=KT)[:, :, a * P:(a + 1) * P]
            if n < Z1:
                return r.rearrange("p (c kv a d) -> p c kv a d", c=KT, kv=2, a=2)[:, :, :, a, :]
            if n < 20:
                return r.rearrange("p (c n) -> p c n", c=4)[:, :, a * 256:(a + 1) * 256]
            return r[:, 0:D].rearrange("p (c n) -> p c n", c=4)

        def raw_unit2(n):
            r, a = raw[:, (n // 2) % 2, :], n % 2
            return r.rearrange("p (c n) -> p c n", c=KT)[:, :, a * P:(a + 1) * P]

        def like_unit1(w, n):
            if n < 10:
                return w[:, :].rearrange("p (c n) -> p c n", c=KT)
            if n < Z1:
                return w[:, :].rearrange("p (c kv d) -> p c kv d", c=KT, kv=2)
            return w[:, :].rearrange("p (c n) -> p c n", c=4)

        def like_unit2(w):
            return w[:, :].rearrange("p (c n) -> p c n", c=KT)

        def scores_of(r, m):
            t = scores_a if r % 2 == 0 else aux
            return t[m, :, :].rearrange("p kv (j n) -> p (kv j) n", j=2)

        def flat(t, n):
            return t[:, 0:LT * n]

        SQUARES = [(), (), (0, 1), (2,), (3, 4), (5, 6), (7,)]
        mlp = Block1(NB1 + 1)
        mlp.n = B2

        def x_rows(blk, r):
            if r < 2:
                return xrow[0:blk.xr, r, :]
            return (av, ix)[r - 2][0:blk.xr, 0:D]

        def y_tiles(r, tail):
            spare = hnext[:, :, :].rearrange("p c n -> p (c n)")
            if tail and r:
                return (aux, scores_a, results, aux)[r][0:YR, :, :], spare[0:YR, (r - 1) * D:r * D]
            return aux[0:YR, :, :], yout[0:YR, :]

        def pair(t, n, h):
            return t[:, 2 * h * n:2 * (h + 1) * n]

        def tiles(t, n):
            return t[:, 0:LT * n].rearrange("p (j n) -> p j n", j=LT)

        @block.sync
        def _(sp):
            def load_group1(g):
                s = g % 2
                if g < 5:
                    dst, cols = raw[:, s, :].rearrange("p (c n) -> p c n", c=KT), slice(UNIT_COLS[g], UNIT_COLS[g] + 256)
                    for c in (slice(0, 4), slice(4, 8)):
                        sp.dma_start(dst[:, c, :], win_v[:, c, cols]).then_inc(raw_in[s], 16)
                elif g < 7:
                    dst = raw[:, s, :].rearrange("p (c kv n) -> p c kv n", c=KT, kv=2)
                    for kv in range(2):
                        col = kv * 256 + (g - 5) * P
                        sp.dma_start(dst[:, :, kv, :], win_v[:, :, col:col + P]).then_inc(raw_in[s], 16)
                elif g < 9:
                    dst, cols = raw[:, s, :].rearrange("p (c n) -> p c n", c=LT), slice((g - 7) * 512, (g - 6) * 512)
                    for c in (slice(0, 2), slice(2, 4)):
                        sp.dma_start(dst[:, c, :], wout_lru[:, c, cols]).then_inc(raw_in[s], 16)
                else:
                    width = 512 if g == 9 else 256
                    at = 0 if g == 9 else 512 + (g - 10) * 256
                    dst = raw[:, s, 0:4 * width].rearrange("p (c n) -> p c n", c=4)
                    for kv in range(2):
                        sp.dma_start(dst[kv * HEAD:(kv + 1) * HEAD, :, :], wout_attn[kv][:, :, at:at + width])\
                          .then_inc(raw_in[s], 16)

            def load_group2(g):
                dst = raw[:, g % 2, :].rearrange("p (c n) -> p c n", c=KT)
                if g < 16:
                    source = wup_v[:, :, g * 256:(g + 1) * 256]
                else:
                    dp, kq = (g - 16) // 4, (g - 16) % 4
                    source = wdown_v[kq][:, :, dp * 256:(dp + 1) * 256]
                for c in (slice(0, 4), slice(4, 8)):
                    sp.dma_start(dst[:, c, :], source[:, c, :]).then_inc(raw_in[g % 2], 16)

            def load_x(blk, r):
                if not blk.first:
                    rows = bass.ds(FIRST + (blk.b - 1) * B1 + r * XR, XR)
                    sp.dma_start(x_rows(blk, r), xp[rows, :]).then_inc(x_in[r], 16)
                elif r < 2:
                    sp.dma_start(x_rows(blk, r), xp[r * XR0:(r + 1) * XR0, :]).then_inc(x_in[r], 16)
                else:
                    rest = FIRST - 2 * XR0
                    sp.dma_start(x_rows(blk, 2)[0:rest, :], xp[2 * XR0:FIRST, :]).then_inc(x_in[2], 16)
                    sp.dma_start(x_rows(blk, 2)[rest:XR0, :], xs[:, :]).then_inc(x_in[2], 16)

            first = Block1(0)
            load_x(first, 0)
            for at, rows, source in (
                    (V_GMIX, 8, norm_mix_g[0]), (V_GFFN, 8, norm_ffn_g[0]),
                    (V_CW, 16, conv_w[0].rearrange("t n -> (t n)")), (V_CB, 4, conv_b[0]),
                    (V_BA, 4, gate_a_b[0]), (V_BX, 4, gate_x_b[0]), (V_LAM, 4, lru_lambda[0]),
                    (V_SC, 12, state_conv[0, 0].rearrange("t n -> (t n)")), (V_SL, 4, state_lru[0, 0])):
                sp.dma_start(vrows[at:at + rows, :], source.rearrange("(r p) -> r p", p=P)).then_inc(vec_in, 16)
            load_x(first, 1)
            load_x(first, 2)
            load_group1(0)
            sp.dma_start(sink8[:, :], attn_sinks.to_broadcast([P, 8])).then_inc(const_in, 16)
            sp.wait_ge(const_set, 3)
            for g, w in enumerate((gate_a_w, gate_x_w)):
                heads = w[0].rearrange("(j h) a b -> h a j b", h=2)
                for hh in range(2):
                    s = slice(hh * HEAD, (hh + 1) * HEAD)
                    sp.dma_start(gate_w[s, g, :, s], heads[hh]).then_inc(const_in, 16)
            sp.dma_start(cache_rows[:, 0, :], cache_k[0, 0, CHUNK:WINDOW].rearrange("s h d -> s (h d)")).then_inc(cache_in, 16)
            sp.dma_start(cache_rows[:, 1, :], cache_v[0, 0, CHUNK:WINDOW].rearrange("s h d -> s (h d)")).then_inc(cache_in, 16)
            load_group1(1)
            for new, old in ((nk_sample, cache_k), (nv_sample, cache_v)):
                sp.dma_start(new[0, 0, 0:WINDOW - SAMPLE].rearrange("s h d -> s (h d)"),
                             old[0, 0, SAMPLE:WINDOW].rearrange("s h d -> s (h d)")).then_inc(small_out, 16)

            def mix_block(blk):
                units, uses = blk.before(U1), blk.before(USES)
                nxt = blk.next()
                for q in range(12):
                    sp.wait_ge(w_lo_done, units + (2 * q + 2 if q < 10 else q + 11))
                    if q + 2 < 12:
                        load_group1(q + 2)
                    elif nxt:
                        load_group1(q - 10)
                    else:
                        load_group2(q - 10)
                    if blk.last and q == 7:
                        sp.wait_ge(freed, 2 + uses + Z1)
                        sp.wait_ge(h_stored, blk.before(32, 64))
                        sp.dma_start(hnext[:, :, :], h_dram[:, :, 0:B2]).then_inc(hnext_in, 16)
                    if nxt and q == 2:
                        load_x(nxt, 0)
                        load_x(nxt, 1)
                    if nxt and q == 7:
                        sp.wait_ge(mixed, blk.before(2) + 2)
                        load_x(nxt, 2)
                        load_x(nxt, 3)
                for half in range(2):
                    d = slice(4 * half, 4 * half + 4)
                    sp.wait_ge(freed, 2 + uses + Z1 + 8 + 4 * half + 4)
                    if blk.first:
                        sp.dma_start(h_dram[:, d, 0:FIRST], hacc[:, d, 0:FIRST]).then_inc(h_stored, 16)
                        sp.dma_start(h_dram[:, d, SEQ:TOKENS], hacc[:, d, FIRST:FIRST + SAMPLE]).then_inc(h_stored, 16)
                    else:
                        sp.dma_start(h_dram[:, d, bass.ds(FIRST + (blk.b - 1) * B1, B1)], hacc[:, d, :])\
                          .then_inc(h_stored, 16)

            mix_block(first)
            sp.dma_start(nk_sample[0, 0, WINDOW - SAMPLE:WINDOW].rearrange("s h d -> s (h d)"),
                         krow[CHUNK:CHUNK + SAMPLE, 0, :]).then_inc(small_out, 16)
            sp.dma_start(nv_sample[0, 0, WINDOW - SAMPLE:WINDOW].rearrange("s h d -> s (h d)"),
                         vrow[CHUNK:CHUNK + SAMPLE, 4, :]).then_inc(small_out, 16)
            with sp.Fori(1, NB1) as b:
                mix_block(Block1(b))
            mix_block(Block1(NB1, last=True))
            sp.dma_start(nk_prompt[0, 0].rearrange("s h d -> s (h d)"), krow[:, 1, :]).then_inc(small_out, 16)
            sp.dma_start(nv_prompt[0, 0].rearrange("s h d -> s (h d)"), vrow[:, 6, :]).then_inc(small_out, 16)
            sp.wait_ge(state_copied, 1)
            for dst, at, rows in ((nconv_prompt[0, 0].rearrange("t n -> (t n)"), 0, 12),
                                  (nconv_sample[0, 0].rearrange("t n -> (t n)"), 12, 12),
                                  (nlru_prompt[0, 0], 24, 4), (nlru_sample[0, 0], 28, 4)):
                sp.dma_start(dst.rearrange("(r p) -> r p", p=P), state_rows[at:at + rows, :]).then_inc(small_out, 16)
            sp.wait_ge(small_out, 10 * 16)
            sp.wait_ge(h_stored, 64 + 32 * NB1)
            sp.dma_start(hcur[:, :, :], h_dram[:, :, 0:B2]).then_inc(hcur_in, 16)
            sp.dma_start(gfin[:, :], final_norm_g.rearrange("(a n) -> a n", a=1).to_broadcast([P, D])).then_inc(y_stored, 16)

            def store_y(b, r, last=False):
                out = y_tiles(r, last)[1]
                sp.wait_ge(yout_done, 1 + b * 4 + r + 1)
                if last and r == 3:
                    rest = YR - SAMPLE
                    sp.dma_start(y_prompt[0, SEQ - rest:SEQ, :], out[0:rest, :]).then_inc(y_stored, 16)
                    sp.dma_start(y_sample[0], out[rest:YR, :]).then_inc(y_stored, 16)
                else:
                    sp.dma_start(y_prompt[0, bass.ds(b * B2 + r * YR, YR), :], out).then_inc(y_stored, 16)

            def loads(b, lo, hi, more, flush=False, ahead=False):
                for q in range(lo, hi):
                    sp.wait_ge(w_lo_done, G1 + b * U2 + 2 * q + 2)
                    if q + 2 < 32 or more:
                        load_group2((q + 2) % 32)
                    if ahead and q == 1:
                        sp.wait_ge(hn_done, 8 * b + 8)
                        sp.dma_start(hnext[:, :, :], h_dram[:, :, bass.ds((b + 1) * B2, B2)]).then_inc(hnext_in, 16)
                    if flush and q in (2, 4, 5, 7):
                        store_y(b - 1, (2, 4, 5, 7).index(q))
                    if flush and q == 8:
                        sp.wait_ge(yT_ready, 4 * b)
                        sp.dma_start(hcur[:, :, :], h_dram[:, :, bass.ds(b * B2, B2)]).then_inc(hcur_in, 16)

            loads(0, 0, 16, True, ahead=True)
            with sp.Fori(0, NB2 - 2) as b:
                loads(b, 16, 32, True)
                loads(b + 1, 0, 16, True, flush=True, ahead=True)
            loads(NB2 - 2, 16, 32, True)
            loads(NB2 - 1, 0, 16, True, flush=True)
            loads(NB2 - 1, 16, 32, False)
            for r in range(4):
                store_y(NB2 - 1, r, last=True)
            sp.wait_ge(y_stored, 16 + 16 * (4 * NB2 + 1))

        @block.gpsimd
        def _(pool):
            nc.gpsimd.memset(ident[:, :], 0.0).then_inc(const_set, 1)
            pool.wait_ge(const_set, 1)
            nc.gpsimd.affine_select(out=ident[:, :], in_=ident[:, :], compare_op=ALU.not_equal, fill=1.0, base=0,
                                    pattern=[[-1, P]], channel_multiplier=1).then_inc(const_set, 1)
            nc.gpsimd.memset(gate_w[:, :, :, :], 0.0).then_inc(const_set, 1)
            nc.gpsimd.memset(ones[:, :], 1.0).then_inc(const_set, 1)

            def add_square(blk, c):
                sums = blk.before(7)
                pool.wait_ge(x_sq, blk.before(8) + c + 1)
                if c == 1:
                    nc.gpsimd.tensor_tensor(sumsq[:, 0:blk.n], sq[:, 0, 0:blk.n], sq[:, 1, 0:blk.n], ALU.add)\
                      .then_inc(sum_done, 1)
                else:
                    pool.wait_ge(sum_done, sums + c - 1)
                    nc.gpsimd.tensor_tensor(sumsq[:, 0:blk.n], sumsq[:, 0:blk.n], sq[:, c % 2, 0:blk.n], ALU.add)\
                      .then_inc(sum_done, 1)

            def sum_squares(blk):
                for c in range(1, KT):
                    add_square(blk, c)

            def mix_block(blk):
                n = blk.n
                for h in range(2):
                    pool.wait_ge(sig_done, blk.before(8) + 4 * h + 4)
                    nc.gpsimd.tensor_tensor(pair(ix, n, h), pair(ix, n, h), pair(xc, n, h), ALU.mult).then_inc(ix_done, 1)
                for h in range(2):
                    pool.wait_ge(ix_done, blk.before(2) + h + 1)
                    pool.wait_ge(drive, blk.before(2) + h + 1)
                    nc.gpsimd.tensor_tensor(pair(ix, n, h), pair(ix, n, h), pair(rt, n, h), ALU.mult).then_inc(scan_in, 1)
                for r, (_, qn, _, nk) in enumerate(blk.rounds):
                    pool.wait_ge(share_done, blk.before(7, 5) + r + 1)
                    m = slice(0, 2 * qn)
                    share = soft[m, r % 2, 3, :].rearrange("p (a o) -> p a o", o=1).to_broadcast([2 * qn, 4, nk])
                    nc.gpsimd.tensor_tensor(prob[m, r % 2, :, :nk], prob[m, r % 2, :, :nk], share, ALU.mult).then_inc(probs_done, 1)
                    if blk.last and r:
                        for c in SQUARES[r - 1]:
                            if c:
                                add_square(mlp, c)
                if blk.last:
                    add_square(mlp, KT - 1)
                else:
                    sum_squares(blk.next())

            sum_squares(Block1(0))
            mix_block(Block1(0))
            with pool.Fori(1, NB1) as b:
                mix_block(Block1(b))
            mix_block(Block1(NB1, last=True))

            def sum_squares2(b):
                chain = (b - 1) * 8
                pool.wait_ge(hnext_in, 16 * b + 16)
                for c in range(KT):
                    if c == 0:
                        nc.gpsimd.tensor_tensor(sumsq2[:, :], hnext[:, 0, :], hnext[:, 0, :], ALU.mult).then_inc(pool_chain, 1)
                        pool.wait_ge(pool_chain, chain + 1)
                    else:
                        if c > 1:
                            pool.wait_ge(sum2_done, (b - 1) * 7 + c - 1)
                        nc.gpsimd.tensor_tensor(sq2[:, :], hnext[:, c, :], hnext[:, c, :], ALU.mult).then_inc(pool_chain, 1)
                        pool.wait_ge(pool_chain, chain + c + 1)
                        nc.gpsimd.tensor_tensor(sumsq2[:, :], sumsq2[:, :], sq2[:, :], ALU.add).then_inc(sum2_done, 1)

            with pool.Fori(1, NB2) as b:
                sum_squares2(b)

        @block.scalar
        def _(act):
            chain = Chain(act, act_chain)

            def split1(blk, n):
                g = load_of1(n % U1)
                loads = blk.before(L1) + (L1 if n >= U1 else 0)
                act.wait_ge(raw_in[g % 2], 32 * (loads + g // 2 + 1))
                nc.scalar.activation(like_unit1(w_hi[n % 2], n % U1), raw_unit1(n % U1), ACT.Copy).then_inc(w_hi_done, 1)

            def split2(b, n):
                g = (n % U2) // 2
                loads = L1 * (NB1 + 1) + b * L2 + (L2 if n >= U2 else 0)
                act.wait_ge(raw_in[g % 2], 32 * (loads + g // 2 + 1))
                nc.scalar.activation(like_unit2(w_hi[n % 2]), raw_unit2(n % U2), ACT.Copy).then_inc(w_hi_done, 1)

            def step1(blk, n):
                act.wait_ge(ready, blk.before(USES) + use_after(n))
                if n + 2 >= U1 and blk.last:
                    split2(-1, U2 + n + 2 - U1)
                else:
                    split1(blk, n + 2)

            def copy_x(blk, r):
                for half in range(2):
                    act.wait_ge(xt_ready, blk.before(8, 6) + 2 * r + half + 1)
                    c = slice(4 * half, 4 * half + 4)
                    nc.scalar.activation(xT[:, c, r * blk.xr:(r + 1) * blk.xr],
                                         aux[:, half, 0:4 * blk.xr].rearrange("p (c n) -> p c n", c=4), ACT.Copy)\
                      .then_inc(xt_copied, 1)

            def high_x(blk, cs):
                for c in cs:
                    if c == 0:
                        act.wait_ge(xt_copied, blk.before(8, 6) + 2 * blk.tiles)
                    nc.scalar.activation(xg_hi[:, c, 0:blk.n], xT[:, c, 0:blk.n], ACT.Copy,
                                         scale=vec[:, V_GMIX + c:V_GMIX + c + 1]).then_inc(xg_hi_done, 1)

            def square_x(blk, cs):
                for c in cs:
                    if c == 0:
                        act.wait_ge(xt_copied, blk.before(8, 6) + 2 * blk.tiles)
                    if c >= 2:
                        act.wait_ge(sum_done, blk.before(7) + max(1, c - 2))
                    nc.scalar.activation(sq[:, c % 2, 0:blk.n], xT[:, c, 0:blk.n], ACT.Square).then_inc(x_sq, 1)

            def square_h(c):
                if c == 0:
                    act.wait_ge(hnext_in, 16)
                if c >= 2:
                    act.wait_ge(sum_done, mlp.before(7) + max(1, c - 2))
                nc.scalar.activation(sq[:, c % 2, 0:B2], hnext[:, c, :], ACT.Square).then_inc(x_sq, 1)

            def deviation2(b):
                act.wait_ge(sum2_all, b + 1)
                nc.scalar.activation(rstd2[:, :], aux[:, 0, 0:B2], ACT.Sqrt, scale=1.0 / D, bias=eps_t[:, 0:1]).then_inc(std2_done, 1)

            def hn_high(b, c):
                act.wait_ge(hn_done, 8 * b + c + 1)
                nc.scalar.activation(hn_hi[:, c, :], (hn_t, sq2)[c % 2][:, :], ACT.Copy).then_inc(hn_hi_done, 1)

            def exps(blk, r):
                _, qn, _, nk = blk.rounds[r]
                m, t = slice(0, 2 * qn), r % 2
                act.wait_ge(bound_done, blk.before(7, 5) + r + 1)
                if r >= 2:
                    act.wait_ge(pT_ready, blk.before(7, 5) + r - 1)
                for a in range(4):
                    nc.scalar.activation(prob[m, t, a, 0:nk], scores_of(r, m)[:, a, 0:nk], ACT.Exp, scale=SCALE,
                                         bias=soft[m, t, 1, a:a + 1], accum_out=soft[m, t, 2, a:a + 1])
                nc.scalar.activation(soft[m, t, 4, :], soft[m, t, 4, :], ACT.Exp).then_inc(exp_done, 1)

            def copy_pT(blk, r):
                _, qn, _, nk = blk.rounds[r]
                act.wait_ge(pT_ready, blk.before(7, 5) + r + 1)
                nc.scalar.activation(pT[0:nk, r % 2, :, 0:2 * qn],
                                     banks[4][0:nk, :].rearrange("p (a n) -> p a n", a=4)[:, :, 0:2 * qn], ACT.Copy)\
                  .then_inc(pT_copied, 1)

            def attn_high(blk, r):
                q0, qn, _, _ = blk.rounds[r]
                act.wait_ge(o_ready, blk.before(7, 5) + r + 1)
                nc.scalar.activation(mix_hi[:, 0:4, q0:q0 + qn], banks[5][:, 0:4 * qn].rearrange("p (t n) -> p t n", t=4),
                                     ACT.Copy).then_inc(o_hi, 1)

            def deviation1(blk):
                act.wait_ge(sum_all, blk.before(1) + 1)
                nc.scalar.activation(rstd[:, 0:blk.n], aux[:, 0, 0:blk.n], ACT.Sqrt, scale=1.0 / D, bias=eps_t[:, 0:1])\
                  .then_inc(std_done, 1)

            def mix_block(blk):
                n, rounds = blk.n, len(blk.rounds)
                nxt = blk.next()
                if not blk.first:
                    deviation1(blk)
                for u in range(Z1):
                    step1(blk, u)
                    if u == 0 and blk.first:
                        deviation1(blk)
                    if u == 1 and blk.first:
                        act.wait_ge(cache_t, 1)
                        nc.scalar.activation(kT[:, K_SAMPLE:K_SAMPLE + CHUNK], aux[:, 1, 0:CHUNK], ACT.Copy)\
                          .then_inc(cache_copied, 1)
                        nc.scalar.activation(vT[:, K_SAMPLE:K_SAMPLE + CHUNK], aux[:, 1, CHUNK:2 * CHUNK], ACT.Copy)\
                          .then_inc(cache_copied, 1)
                    if u < LT:
                        act.wait_ge(freed, 2 + blk.before(USES) + u + 1)
                        for a, o, m in blk.segs:
                            nc.scalar.activation(tiles(xc, n)[:, u, o:o + m], uT[:, u, a:a + m], ACT.Identity,
                                                 scale=vec[:, V_CW + u:V_CW + u + 1],
                                                 bias=vec[:, V_CB + u:V_CB + u + 1]).then_inc(tap0, 1)
                    if 2 <= u < 6:
                        j = u - 2
                        for g, (dst, at) in enumerate(((rt, V_BA), (ix, V_BX))):
                            act.wait_ge(gates_ready, blk.before(8) + 2 * j + g + 1)
                            nc.scalar.activation(tiles(dst, n)[:, j, :], aux[:, g, 0:n], ACT.Sigmoid,
                                                 bias=vec[:, at + j:at + j + 1]).then_inc(sig_done, 1)
                    if u in (6, 7):
                        act.wait_ge(sig_done, blk.before(8) + 4 * (u - 6) + 4)
                        for j in (2 * (u - 6), 2 * (u - 6) + 1):
                            nc.scalar.activation(tiles(av, n)[:, j, :], tiles(rt, n)[:, j, :], ACT.Exp,
                                                 scale=decay[:, 0, j:j + 1]).then_inc(act_chain, 1)
                            chain.n += 1
                    if u in (7, 8):
                        act.wait_ge(act_chain, chain.base + chain.n)
                        for j in (2 * (u - 7), 2 * (u - 7) + 1):
                            nc.scalar.activation(tiles(rt, n)[:, j, :], tiles(rt, n)[:, j, :], ACT.Tanh,
                                                 scale=decay[:, 1, j:j + 1]).then_inc(tanh_done, 1)
                    if u == 9:
                        for h in range(2):
                            act.wait_ge(newton, blk.before(2) + h + 1)
                            nc.scalar.activation(pair(rt, n, h), pair(rt, n, h), ACT.Sqrt, scale=4.0).then_inc(sqrt_done, 1)
                    if u == 10:
                        nc.scalar.activation(flat(gT, n), flat(gT, n), ACT.Gelu_apprx_tanh).then_inc(gelu_done, 1)
                    if u == 11:
                        act.wait_ge(vwin_ready, blk.before(2) + 2)
                        if blk.first:
                            for r, (_, _, _, nk) in enumerate(blk.rounds):
                                nc.scalar.activation(vrow[0:nk, r, :], aux[0:nk, r // 4, (r % 4) * P:(r % 4 + 1) * P],
                                                     ACT.Copy).then_inc(vwin_copied, 1)
                            nc.scalar.activation(krow[0:CHUNK + SAMPLE, 0, :], aux[0:CHUNK + SAMPLE, 1, P:2 * P],
                                                 ACT.Copy).then_inc(vwin_copied, 1)
                        else:
                            act.wait_ge(small_out, 4 * 16)
                            nc.scalar.activation(vrow[:, 0:4, :], aux[:, 0, :].rearrange("p (r n) -> p r n", r=4),
                                                 ACT.Copy).then_inc(vwin_copied, 1)
                            nc.scalar.activation(vrow[:, 4:7, :], aux[:, 1, 0:3 * P].rearrange("p (r n) -> p r n", r=3),
                                                 ACT.Copy).then_inc(vwin_copied, 1)
                            if blk.last:
                                nc.scalar.activation(krow[:, 1, :], aux[:, 1, 3 * P:4 * P], ACT.Copy).then_inc(vwin_copied, 1)
                    if u in (11, 12):
                        h = u - 11
                        act.wait_ge(mixed, blk.before(2) + h + 1)
                        nc.scalar.activation(mix_hi[:, 4 + 2 * h:6 + 2 * h, 0:n], tiles(rt, n)[:, 2 * h:2 * h + 2, :],
                                             ACT.Copy).then_inc(lru_hi, 1)
                exps(blk, 0)
                for r in range(rounds):
                    if r + 1 < rounds:
                        exps(blk, r + 1)
                    if r:
                        attn_high(blk, r - 1)
                    copy_pT(blk, r)
                    if r % 2 == 0 and r < 6:
                        step1(blk, Z1 + r // 2)
                    if blk.last:
                        for c in SQUARES[r]:
                            square_h(c)
                attn_high(blk, rounds - 1)
                if blk.last:
                    step1(blk, Z1 + 3)
                    act.wait_ge(state_t, 1)
                    nc.scalar.activation(state_rows[:, :], aux[0:32, 1, 0:P], ACT.Copy).then_inc(state_copied, 1)
                    deviation2(0)
                    for h in range(4):
                        step1(blk, 18 + h)
                        hn_high(0, 2 * h)
                        hn_high(0, 2 * h + 1)
                else:
                    act.wait_ge(freed, 2 + blk.before(USES) + Z1 + 8)
                    copy_x(nxt, 0)
                    step1(blk, Z1 + 3)
                    copy_x(nxt, 1)
                    copy_x(nxt, 2)
                    step1(blk, 18)
                    copy_x(nxt, 3)
                    for unit, work in ((19, "s0 s1 h0 s2 h1 s3"), (20, "s4 h2 s5 h3 s6 h4"), (21, "s7 h5 h6 h7")):
                        for item in work.split():
                            (square_x if item[0] == "s" else high_x)(nxt, (int(item[1]),))
                        if unit < 21:
                            step1(blk, unit)
                    step1(blk, 21)

            first = Block1(0)
            act.wait_ge(vec_t, 1)
            nc.scalar.activation(vec[:, :], banks[4][:, 0:VROWS], ACT.Copy).then_inc(vec_ready, 1)
            act.wait_ge(setup_done, 1)
            nc.scalar.activation(tiny[:, 2, :], tiny[:, 1, :], ACT.Exp, scale=-1.0).then_inc(decay_e, 1)
            copy_x(first, 0)
            copy_x(first, 1)
            copy_x(first, 2)
            split1(first, 0)
            act.wait_ge(vec_ready, 1)
            for c in range(KT):
                square_x(first, (c,))
                high_x(first, (c,))
                if c == 3:
                    split1(first, 1)
            act.wait_ge(setup_done, 2)
            mix_block(first)
            with act.Fori(1, NB1) as b:
                chain.enter(b - 1, LT)
                mix_block(Block1(b))
            chain.leave(NB1 - 1)
            mix_block(Block1(NB1, last=True))

            def step2(b, n, more=True):
                act.wait_ge(unit_done, b * U2 + n + 1)
                if n + 2 < U2 or more:
                    split2(b, n + 2)

            def y_deviation(b, r, tail=False):
                rows, out = y_tiles(r, tail)
                act.wait_ge(yT_ready, 4 * b + r + 1)
                if not (tail and r):
                    act.wait_ge(y_stored, 16 * (4 * b + r) + 16)
                nc.scalar.activation(out, rows, ACT.Square, accum_out=ystat[0:YR, r, 0:1]).then_inc(act_chain, 1)
                chain.n += 1
                act.wait_ge(act_chain, chain.base + chain.n)
                nc.scalar.activation(ystat[0:YR, r, 1:2], ystat[0:YR, r, 0:1], ACT.Sqrt, scale=1.0 / D, bias=eps_t[0:YR, 0:1])\
                  .then_inc(ystd_done, 1)

            def up(b, flush):
                for j in range(FT):
                    act.wait_ge(unit_done, b * U2 + j + 1)
                    if j >= 2:
                        act.wait_ge(hid_lo_done, 32 * b + j - 1)
                    nc.scalar.activation(act_t[:, j % 2, :], banks[j % 2][:, 0:B2], ACT.Relu).then_inc(relu_done, 1)
                    split2(b, j + 2)
                    act.wait_ge(relu_done, 32 * b + j + 1)
                    nc.scalar.activation(act_t[:, j % 2, :], act_t[:, j % 2, :], ACT.Square).then_inc(sq_done, 1)
                    if flush and j in (2, 5, 8, 11):
                        y_deviation(b - 1, j // 3)

            def down(b, prepare, more=True):
                for m in range(32):
                    step2(b, 32 + m, more)
                    if prepare and m == 4:
                        deviation2(b + 1)
                    if prepare and m >= 7 and (m - 7) % 3 == 0 and (m - 7) // 3 < KT:
                        hn_high(b + 1, (m - 7) // 3)

            act.wait_ge(h_stored, 64 + 32 * NB1)
            up(0, False)
            with act.Fori(0, NB2 - 1) as b:
                chain.enter(b, 4)
                down(b, True)
                up(b + 1, True)
            chain.leave(NB2 - 1)
            down(NB2 - 1, False, more=False)
            for r in range(4):
                y_deviation(NB2 - 1, r, tail=True)

        @block.vector
        def _(dve):
            chain = Chain(dve, dve_chain)
            link = chain.link

            def split1(blk, n):
                dve.wait_ge(w_hi_done, blk.before(U1) + n + 1)
                m = n % U1
                nc.vector.tensor_tensor(like_unit1(w_lo[n % 2], m), raw_unit1(m), like_unit1(w_hi[n % 2].bitcast(F32), m),
                                        ALU.subtract).then_inc(w_lo_done, 1)

            def split2(b, n):
                dve.wait_ge(w_hi_done, G1 + b * U2 + n + 1)
                nc.vector.tensor_tensor(like_unit2(w_lo[n % 2]), raw_unit2(n % U2), like_unit2(w_hi[n % 2].bitcast(F32)),
                                        ALU.subtract).then_inc(w_lo_done, 1)

            def next_split(blk, n):
                if n + 2 >= U1 and blk.last:
                    split2(0, n + 2 - U1)
                else:
                    split1(blk, n + 2)

            def low_x(blk, cs):
                n = blk.n
                for c in cs:
                    dve.wait_ge(xg_hi_done, blk.before(8) + c + 1)
                    nc.vector.scalar_tensor_tensor(xg_lo[:, c, 0:n], xT[:, c, 0:n], vec[:, V_GMIX + c:V_GMIX + c + 1],
                                                   xg_hi.bitcast(F32)[:, c, 0:n], ALU.mult, ALU.subtract)\
                      .then_inc(xg_lo_done, 1)

            def take_z(blk, u):
                n, uses = blk.n, blk.before(USES)
                dve.wait_ge(ready, uses + u + 1)
                z = banks[u % 2]
                if u < LT:
                    parts = [(uT[:, u, a + 3:a + 3 + m], o, m) for a, o, m in blk.segs]
                elif u < 2 * LT:
                    parts = [(tiles(gT, n)[:, u - LT, :], 0, n)]
                elif u < 10:
                    t = (kT, vT)[u - 8]
                    if blk.first:
                        parts = [(t[:, CHUNK:CHUNK + FIRST], 0, FIRST),
                                 (t[:, K_SAMPLE + CHUNK:K_SAMPLE + CHUNK + SAMPLE], FIRST, SAMPLE)]
                    else:
                        parts = [(t[:, CHUNK:CHUNK + B1], 0, B1)]
                else:
                    j, hh = (u - 10) // 2, u % 2
                    m = FIRST if blk.first else B1
                    chunks = qT[:, j, 0:2 * m].rearrange("p (c h q) -> p c h q", h=2, q=CHUNK)[:, :, hh, :]
                    parts = [(chunks, 0, m)]
                    if blk.first:
                        parts.append((qT[:, j, 2 * m + hh * SAMPLE:2 * m + (hh + 1) * SAMPLE], m, SAMPLE))
                for k, (dst, o, m) in enumerate(parts):
                    a, b = z[:, o:o + m], rstd[:, o:o + m]
                    if len(dst.shape) == 3:
                        a, b = (x.rearrange("p (c q) -> p c q", q=CHUNK) for x in (a, b))
                    ins = nc.vector.tensor_tensor(dst, a, b, ALU.mult)
                    if k == len(parts) - 1:
                        ins.then_inc(freed, 1)

            def convolve(blk, j):
                n = blk.n
                dve.wait_ge(tap0, blk.before(4, 8) + len(blk.segs) * (j + 1))
                for t in range(1, TAPS):
                    for k, (a, o, m) in enumerate(blk.segs):
                        x = tiles(xc, n)[:, j, o:o + m]
                        ins = nc.vector.scalar_tensor_tensor(x, uT[:, j, a + t:a + t + m], vec[:, V_CW + 4 * t + j:V_CW + 4 * t + j + 1],
                                                             x, ALU.mult, ALU.add)
                        if k < len(blk.segs) - 1:
                            continue
                        if t < TAPS - 1:
                            link(ins)
                        else:
                            ins.then_inc(conv_done, 1)

            def bound(blk, r):
                _, qn, _, nk = blk.rounds[r]
                s, m = r % 2, slice(0, 2 * qn)
                sk, minus = (sink_s[m, t, :] if qn == SAMPLE else sink[m, t, :] for t in range(2))
                dve.wait_ge(scores_ready, blk.before(7, 5) + r + 1)
                link(nc.vector.tensor_reduce(soft[m, s, 0, :], scores_of(r, m)[:, :, 0:nk], AX_X, ALU.max))
                link(nc.vector.scalar_tensor_tensor(soft[m, s, 1, :], soft[m, s, 0, :], -SCALE, minus, ALU.mult, ALU.min))
                nc.vector.tensor_tensor(soft[m, s, 4, :], sk, soft[m, s, 1, :], ALU.add).then_inc(bound_done, 1)

            def share(blk, r):
                _, qn, _, _ = blk.rounds[r]
                s, m = r % 2, slice(0, 2 * qn)
                dve.wait_ge(exp_done, blk.before(7, 5) + r + 1)
                link(nc.vector.tensor_tensor(soft[m, s, 2, :], soft[m, s, 2, :], soft[m, s, 4, :], ALU.add))
                nc.vector.reciprocal(soft[m, s, 3, :], soft[m, s, 2, :]).then_inc(share_done, 1)

            def attn_low(blk, r):
                q0, qn, _, _ = blk.rounds[r]
                dve.wait_ge(o_hi, blk.before(7, 5) + r + 1)
                nc.vector.tensor_tensor(mix_lo[:, 0:4, q0:q0 + qn], banks[5][:, 0:4 * qn].rearrange("p (t n) -> p t n", t=4),
                                        mix_hi.bitcast(F32)[:, 0:4, q0:q0 + qn], ALU.subtract).then_inc(o_lo, 1)

            def take_out(blk, h):
                n, u, d = blk.n, Z1 + h, h % 8
                dve.wait_ge(ready, blk.before(USES) + u + 1)
                if h == 0 and not blk.first:
                    dve.wait_ge(h_stored, blk.before(32, 64))
                if h == 8:
                    dve.wait_ge(freed, 2 + blk.before(USES) + Z1 + 8)
                other = xT if h < 8 else hacc
                nc.vector.tensor_tensor(hacc[:, d, 0:n], banks[u % 2][:, 0:n], other[:, d, 0:n], ALU.add).then_inc(freed, 1)

            def deviation2(b):
                dve.wait_ge(std2_done, b + 1)
                link(nc.vector.reciprocal(rstd2[:, :], rstd2[:, :]))

            def low2(b, c):
                dve.wait_ge(hn_hi_done, 8 * b + c + 1)
                nc.vector.tensor_tensor(hn_lo[:, c, :], (hn_t, sq2)[c % 2][:, :], hn_hi.bitcast(F32)[:, c, :], ALU.subtract)\
                  .then_inc(hn_lo_done, 1)

            def normalise2(b, c):
                if c >= 2:
                    dve.wait_ge(hn_lo_done, 8 * b + c - 1)
                nc.vector.scalar_tensor_tensor((hn_t, sq2)[c % 2][:, :], hnext[:, c, :], vec[:, V_GFFN + c:V_GFFN + c + 1],
                                               rstd2[:, :], ALU.mult, ALU.mult).then_inc(hn_done, 1)
                if c:
                    low2(b, c - 1)
                if c == KT - 1:
                    low2(b, c)

            def mix_block(blk):
                n, rounds = blk.n, len(blk.rounds)
                nxt = blk.next()
                end = FIRST if blk.first else B1
                dve.wait_ge(std_done, blk.before(1) + 1)
                link(nc.vector.reciprocal(rstd[:, 0:n], rstd[:, 0:n]))
                for u in range(Z1):
                    take_z(blk, u)
                    if u < Z1 - 1:
                        next_split(blk, u)
                    if u < LT:
                        convolve(blk, u)
                    if u == LT:
                        dve.wait_ge(conv_done, blk.before(4) + 4)
                        if blk.first:
                            link(nc.vector.tensor_copy(state[:, 12:24].rearrange("p (t j) -> p j t", t=3),
                                                       uT[:, :, FIRST + SAMPLE + 3:FIRST + SAMPLE + 6]))
                        if blk.last:
                            link(nc.vector.tensor_copy(state[:, 0:12].rearrange("p (t j) -> p j t", t=3), uT[:, :, B1:B1 + 3]))
                        link(nc.vector.tensor_copy(uT[:, :, 0:3], uT[:, :, end:end + 3]))
                    if u in (7, 8):
                        h = u - 7
                        q0, t, m = (pair(x, n, h) for x in (av, rt, xc))
                        dve.wait_ge(tanh_done, blk.before(4) + 2 * h + 2)
                        link(nc.vector.tensor_scalar(q0, q0, 0.5, 0.5, ALU.mult, ALU.add))
                        dve.wait_ge(ix_done, blk.before(2) + h + 1)
                        nc.vector.scalar_tensor_tensor(m, t, 1.0, q0, ALU.add, ALU.mult).then_inc(newton, 1)
                        dve.wait_ge(newton, blk.before(2) + h + 1)
                        link(nc.vector.scalar_tensor_tensor(q0, m, 2.0, q0, ALU.subtract, ALU.mult))
                    if u in (9, 10):
                        h = u - 9
                        dve.wait_ge(sqrt_done, blk.before(2) + h + 1)
                        nc.vector.scalar_tensor_tensor(pair(rt, n, h), pair(av, n, h), -1.0, pair(rt, n, h), ALU.mult, ALU.mult)\
                          .then_inc(drive, 1)
                        dve.wait_ge(drive, blk.before(2) + h + 1)
                        link(nc.vector.tensor_scalar(pair(av, n, h), pair(av, n, h), -2.0, -1.0, ALU.mult, ALU.add))
                    if u in (10, 11):
                        h = u - 10
                        dve.wait_ge(scan_in, blk.before(2) + h + 1)
                        for j in (2 * h, 2 * h + 1):
                            for s, (_, o, m) in enumerate(blk.segs):
                                if not blk.first:
                                    start = carry[:, j:j + 1]
                                else:
                                    start = vec[:, V_SL + j:V_SL + j + 1] if s else 0.0
                                x = tiles(xc, n)[:, j, o:o + m]
                                ins = nc.vector.tensor_tensor_scan(x, tiles(av, n)[:, j, o:o + m], tiles(ix, n)[:, j, o:o + m],
                                                                   start, ALU.mult, ALU.add)
                        link(ins)
                    if u in (11, 12):
                        h = u - 11
                        dve.wait_ge(gelu_done, blk.before(1) + 1)
                        nc.vector.tensor_tensor(pair(rt, n, h), pair(gT, n, h), pair(xc, n, h), ALU.mult).then_inc(mixed, 1)
                    if u == 12:
                        link(nc.vector.tensor_copy(carry[:, :].rearrange("p (j o) -> p j o", o=1), tiles(xc, n)[:, :, end - 1:end]))
                        if blk.first:
                            link(nc.vector.tensor_copy(state[:, 28:32].rearrange("p (j o) -> p j o", o=1), tiles(xc, n)[:, :, n - 1:n]))
                        if blk.last:
                            nc.vector.tensor_copy(state[:, 24:28], carry[:, :]).then_inc(state_set, 1)
                for h in range(2):
                    dve.wait_ge(lru_hi, blk.before(2) + h + 1)
                    nc.vector.tensor_tensor(mix_lo[:, 4 + 2 * h:6 + 2 * h, 0:n], tiles(rt, n)[:, 2 * h:2 * h + 2, :],
                                            mix_hi.bitcast(F32)[:, 4 + 2 * h:6 + 2 * h, 0:n], ALU.subtract).then_inc(lru_lo, 1)
                bound(blk, 0)
                next_split(blk, Z1 - 1)
                take_out(blk, 0)
                for r in range(rounds):
                    share(blk, r)
                    if r + 1 < rounds:
                        bound(blk, r + 1)
                    if r % 2 == 1:
                        next_split(blk, Z1 + r // 2)
                    take_out(blk, r + 1)
                    if r:
                        attn_low(blk, r - 1)
                if blk.first:
                    next_split(blk, Z1 + 2)
                link(nc.vector.tensor_copy(kT[:, 0:CHUNK], kT[:, end:end + CHUNK]))
                nc.vector.tensor_copy(vT[:, 0:CHUNK], vT[:, end:end + CHUNK]).then_inc(halo_done, 1)
                for h in range(rounds + 1, 8):
                    take_out(blk, h)
                attn_low(blk, rounds - 1)
                next_split(blk, Z1 + 3)
                if blk.last:
                    deviation2(0)
                for couple in range(4):
                    take_out(blk, 8 + 2 * couple)
                    take_out(blk, 9 + 2 * couple)
                    next_split(blk, 18 + couple)
                    if blk.last:
                        for c in (2 * couple, 2 * couple + 1):
                            normalise2(0, c)
                    if nxt and couple >= 1:
                        low_x(nxt, range(max(0, 3 * couple - 4), 3 * couple - 1))

            nc.vector.memset(eps_t[:, :], EPS).then_inc(freed, 2)
            link(nc.vector.memset(uT[:, :, 0:3], 0.0))
            link(nc.vector.memset(soft[:, :, :, :], 0.0))
            dve.wait_ge(vec_ready, 1)
            link(nc.vector.tensor_copy(uT[:, :, FIRST + 3:FIRST + 6], vec[:, V_SC:V_SC + 12].rearrange("p (t j) -> p j t", t=3)))
            lam = vec[:, V_LAM:V_LAM + LT]
            neg, mag, e, s1, s2, ser, pos = (tiny[:, k, :] for k in range(7))
            link(nc.vector.tensor_scalar(neg, lam, -1.0, None, ALU.mult))
            nc.vector.tensor_tensor(mag, lam, neg, ALU.max).then_inc(setup_done, 1)
            dve.wait_ge(decay_e, 1)
            link(nc.vector.tensor_scalar(s1, e, 2.0, None, ALU.add))
            link(nc.vector.reciprocal(s1, s1))
            link(nc.vector.tensor_tensor(s1, s1, e, ALU.mult))
            link(nc.vector.tensor_tensor(s2, s1, s1, ALU.mult))
            link(nc.vector.tensor_scalar(ser, s2, 1.0 / 17, 1.0 / 15, ALU.mult, ALU.add))
            for k in (13, 11, 9, 7, 5, 3, 1):
                link(nc.vector.tensor_tensor(ser, ser, s2, ALU.mult))
                link(nc.vector.tensor_scalar(ser, ser, 1.0 / k, None, ALU.add))
            link(nc.vector.tensor_tensor(ser, ser, s1, ALU.mult))
            link(nc.vector.tensor_scalar(pos, neg, 0.0, None, ALU.max))
            link(nc.vector.scalar_tensor_tensor(pos, ser, 2.0, pos, ALU.mult, ALU.add))
            nc.vector.tensor_scalar(decay[:, 0, :], pos, -8.0, None, ALU.mult)
            nc.vector.tensor_scalar(decay[:, 1, :], pos, 4.0, None, ALU.mult).then_inc(setup_done, 1)
            first = Block1(0)
            split1(first, 0)
            low_x(first, range(4))
            split1(first, 1)
            low_x(first, range(4, KT))
            dve.wait_ge(const_in, 5 * 16)
            for hh in range(2):
                s8 = sink8[:, :].rearrange("p (a h) -> p a h", h=2)
                for t, sign in enumerate((1.0, -1.0)):
                    nc.vector.tensor_scalar(sink[hh * HEAD:(hh + 1) * HEAD, t, :], s8[hh * HEAD:(hh + 1) * HEAD, :, hh],
                                            sign, None, ALU.mult)
                    nc.vector.tensor_scalar(sink_s[hh * SAMPLE:(hh + 1) * SAMPLE, t, :],
                                            s8[hh * SAMPLE:(hh + 1) * SAMPLE, :, hh], sign, None, ALU.mult)
            mix_block(first)
            with dve.Fori(1, NB1) as b:
                chain.enter(b - 1, CHAIN1)
                mix_block(Block1(b))
            chain.leave(NB1 - 1)
            mix_block(Block1(NB1, last=True))

            def write_y(b, r, tail=False):
                rows, out = y_tiles(r, tail)
                dve.wait_ge(ystd_done, 4 * b + r + 1)
                link(nc.vector.reciprocal(ystat[0:YR, r, 2:3], ystat[0:YR, r, 1:2]))
                nc.vector.scalar_tensor_tensor(out.rearrange("p (a n) -> p a n", a=2), rows,
                                               ystat[0:YR, r, 2:3], gfin[0:YR, :].rearrange("p (a n) -> p a n", a=2),
                                               ALU.mult, ALU.mult).then_inc(yout_done, 1)

            def up(b, flush):
                for j in range(FT):
                    split2(b, j + 2)
                    dve.wait_ge(sq_done, 32 * b + j + 1)
                    nc.vector.tensor_copy(hid_hi[:, j, :], act_t[:, j % 2, :]).then_inc(hid_hi_done, 1)
                    dve.wait_ge(hid_hi_done, 32 * b + j + 1)
                    nc.vector.tensor_tensor(hid_lo[:, j, :], act_t[:, j % 2, :], hid_hi.bitcast(F32)[:, j, :], ALU.subtract)\
                      .then_inc(hid_lo_done, 1)
                    if flush and j in (2, 5, 8, 11):
                        write_y(b - 1, j // 3)

            def down(b, prepare, more=True):
                dve.wait_ge(hcur_in, 16 * b + 16)
                for m in range(32):
                    if m + 34 < U2 or more:
                        split2(b, m + 34)
                    if (m % 8) // 2 == 3:
                        d = 2 * (m // 8) + m % 2
                        dve.wait_ge(unit_done, b * U2 + 32 + m + 1)
                        nc.vector.tensor_tensor(hcur[:, d, :], banks[2 + (d // 2) % 2 * 2 + d % 2][:, 0:B2], hcur[:, d, :], ALU.add)\
                          .then_inc(y_done, 1)
                    if prepare and m == 4:
                        deviation2(b + 1)
                    if prepare and m >= 7 and (m - 7) % 3 == 0 and (m - 7) // 3 < KT:
                        normalise2(b + 1, (m - 7) // 3)

            dve.wait_ge(h_stored, 64 + 32 * NB1)
            dve.wait_ge(small_out, 10 * 16)
            nc.vector.memset(ystat[:, :, :], 0.0).then_inc(yout_done, 1)
            up(0, False)
            with dve.Fori(0, NB2 - 1) as b:
                chain.enter(b, 5)
                down(b, True)
                up(b + 1, True)
            chain.leave(NB2 - 1)
            down(NB2 - 1, False, more=False)
            for r in range(4):
                write_y(NB2 - 1, r, tail=True)

        @block.tensor
        def _(pe):
            def product(out, w, wcols, hi, lo, ks, start=True, stop=True):
                for i, (kw, kx) in enumerate(ks):
                    for part, (a, x) in enumerate(((w_hi, hi), (w_hi, lo), (w_lo, hi))):
                        wt = a[w][:, kw * wcols[0] + wcols[1]:kw * wcols[0] + wcols[1] + P]
                        last = nc.tensor.matmul(out, wt, x(kx), start=(start and i == 0 and part == 0),
                                                stop=(stop and i == len(ks) - 1 and part == 2))
                return last

            def transpose_x(blk, r):
                if blk.first and r == 0:
                    pe.wait_ge(const_set, 2)
                in_first = (1, 1, 2, 0)[r]
                pe.wait_ge(x_in[r], 16 * (in_first if blk.first else blk.before(1, in_first) + 1))
                for half in range(2):
                    if r:
                        pe.wait_ge(xt_copied, blk.before(8, 6) + 2 * (r - 1) + half + 1)
                    elif not blk.first:
                        pe.wait_ge(vwin_copied, 6 + (blk.b - 1) * 2)
                    for c in range(4):
                        last = nc.tensor.transpose(aux[:, half, c * blk.xr:(c + 1) * blk.xr],
                                                   x_rows(blk, r)[:, (4 * half + c) * P:(4 * half + c + 1) * P],
                                                   ident[0:blk.xr, 0:blk.xr])
                    last.then_inc(xt_ready, 1)

            def scores(blk, r, js=(0, 1)):
                q0, qn, k0, nk = blk.rounds[r]
                if r >= 2:
                    pe.wait_ge(exp_done, blk.before(7, 5) + r - 1)
                for j in js:
                    for kv in range(2):
                        m = slice(kv * HEAD, (kv + 1) * HEAD)
                        last = nc.tensor.matmul(scores_of(r, slice(0, 2 * qn))[:, 2 * kv + j, 0:nk],
                                                qT[m, j, 2 * q0:2 * (q0 + qn)], kT[m, k0:k0 + nk], start=True, stop=True)
                    if j == 1:
                        last.then_inc(scores_ready, 1)

            def transpose_p(blk, r):
                _, qn, _, nk = blk.rounds[r]
                pe.wait_ge(probs_done, blk.before(7, 5) + r + 1)
                if r:
                    pe.wait_ge(pT_copied, blk.before(7, 5) + r)
                for a in range(4):
                    last = nc.tensor.transpose(banks[4][0:nk, a * P:a * P + 2 * qn], prob[0:2 * qn, r % 2, a, 0:nk],
                                               ident[0:2 * qn, 0:2 * qn])
                last.then_inc(pT_ready, 1)

            def attend(blk, r):
                _, qn, _, nk = blk.rounds[r]
                pe.wait_ge(pT_copied, blk.before(7, 5) + r + 1)
                if r:
                    pe.wait_ge(o_lo, blk.before(7, 5) + r)
                for kv in range(2):
                    m = slice(kv * HEAD, (kv + 1) * HEAD)
                    last = nc.tensor.matmul(banks[5][m, 0:4 * qn], vrow[0:nk, r, m], pT[0:nk, r % 2, 2 * kv:2 * kv + 2, 0:2 * qn],
                                            start=True, stop=True)
                last.then_inc(o_ready, 1)

            def out_half(blk, h):
                n, u, unit = blk.n, Z1 + h, Z1 + h // 2
                if h % 2 == 0:
                    pe.wait_ge(w_lo_done, blk.before(U1) + unit + 1)
                pe.wait_ge(freed, blk.before(USES) + u + 1)
                if h == 8:
                    pe.wait_ge(o_lo, blk.before(7, 5) + len(blk.rounds))
                k0 = 4 if h < 8 else 0
                for kk in ((0, 1), (2, 3)):
                    if h == 0:
                        pe.wait_ge(lru_lo, blk.before(2) + kk[0] // 2 + 1)
                    last = product(banks[u % 2][:, 0:n], unit % 2, (256, (h % 2) * P), lambda k: mix_hi[:, k, 0:n],
                                   lambda k: mix_lo[:, k, 0:n], [(k, k0 + k) for k in kk], start=kk[0] == 0, stop=kk[0] == 2)
                last.then_inc(ready, 1)

            def sum_all2(b):
                first = isinstance(b, int) and b == 0
                if first:
                    pe.wait_ge(sum_done, mlp.before(7) + 7)
                else:
                    pe.wait_ge(sum2_done, 7 * b)
                nc.tensor.matmul(aux[:, 0, 0:B2], ones[:, :], sumsq[:, 0:B2] if first else sumsq2[:, :],
                                 start=True, stop=True).then_inc(sum2_all, 1)

            def sum_all1(blk):
                pe.wait_ge(sum_done, blk.before(7) + 7)
                if blk.first:
                    pe.wait_ge(const_set, 4)
                nc.tensor.matmul(aux[:, 0, 0:blk.n], ones[:, :], sumsq[:, 0:blk.n], start=True, stop=True).then_inc(sum_all, 1)

            def mix_block(blk):
                n = blk.n
                uses, units = blk.before(USES), blk.before(U1)
                nxt = blk.next()
                if not blk.first:
                    sum_all1(blk)
                for u in range(Z1):
                    pe.wait_ge(w_lo_done, units + u + 1)
                    pe.wait_ge(freed, uses + u + 1)
                    if u == 0:
                        for c in range(KT):
                            pe.wait_ge(xg_lo_done, blk.before(8) + c + 1)
                            last = product(banks[0][:, 0:n], 0, (P, 0), lambda k: xg_hi[:, k, 0:n],
                                           lambda k: xg_lo[:, k, 0:n], [(c, c)], start=c == 0, stop=c == KT - 1)
                    else:
                        last = product(banks[u % 2][:, 0:n], u % 2, (P, 0), lambda k: xg_hi[:, k, 0:n],
                                       lambda k: xg_lo[:, k, 0:n], [(c, c) for c in range(KT)])
                    last.then_inc(ready, 1)
                    if u == 0 and blk.first:
                        sum_all1(blk)
                    if u == 1 and blk.first:
                        pe.wait_ge(cache_in, 32)
                        nc.tensor.transpose(aux[:, 1, 0:CHUNK], cache_rows[:, 0, :], ident[0:CHUNK, 0:CHUNK])
                        nc.tensor.transpose(aux[:, 1, CHUNK:2 * CHUNK], cache_rows[:, 1, :], ident[0:CHUNK, 0:CHUNK])\
                          .then_inc(cache_t, 1)
                        pe.wait_ge(const_in, 5 * 16)
                    if 2 <= u < 6:
                        j = u - 2
                        pe.wait_ge(conv_done, blk.before(4) + j + 1)
                        for g in range(2):
                            if j:
                                pe.wait_ge(sig_done, blk.before(8) + 2 * j - 1 + g)
                            elif g == 0:
                                pe.wait_ge(std_done, blk.before(1) + 1)
                            elif blk.first:
                                pe.wait_ge(cache_copied, 2)
                            nc.tensor.matmul(aux[:, g, 0:n], gate_w[:, g, j, :], tiles(xc, n)[:, j, :], start=True, stop=True)\
                              .then_inc(gates_ready, 1)
                    if u == 10:
                        pe.wait_ge(freed, 2 + uses + 10)
                        pe.wait_ge(sig_done, blk.before(8) + 8)
                        if not blk.first:
                            pe.wait_ge(halo_done, blk.before(1))
                        for g in range(2):
                            for r, (_, _, k0, nk) in list(enumerate(blk.rounds))[4 * g:4 * g + 4]:
                                last = nc.tensor.transpose(aux[0:nk, g, (r % 4) * P:(r % 4 + 1) * P], vT[:, k0:k0 + nk], ident[:, :])
                            if g == 1 and blk.first:
                                last = nc.tensor.transpose(aux[0:CHUNK + SAMPLE, 1, P:2 * P],
                                                           kT[:, K_SAMPLE:K_SAMPLE + CHUNK + SAMPLE], ident[:, :])
                            if g == 1 and blk.last:
                                last = nc.tensor.transpose(aux[:, 1, 3 * P:4 * P], kT[:, B1 - CHUNK:B1 + CHUNK], ident[:, :])
                            last.then_inc(vwin_ready, 1)
                pe.wait_ge(freed, 2 + uses + Z1 - 1)
                scores(blk, 0, (0,))
                pe.wait_ge(vwin_copied, 6 if blk.first else 6 + (blk.b - 1) * 2 + 2 + blk.last)
                scores(blk, 1, (0,))
                pe.wait_ge(freed, 2 + uses + Z1)
                scores(blk, 0, (1,))
                scores(blk, 1, (1,))
                out_half(blk, 0)
                for r in range(len(blk.rounds)):
                    out_half(blk, r + 1)
                    if r:
                        attend(blk, r - 1)
                    transpose_p(blk, r)
                    if r + 2 < len(blk.rounds):
                        scores(blk, r + 2)
                for h in range(len(blk.rounds) + 1, 8):
                    out_half(blk, h)
                if nxt:
                    transpose_x(nxt, 0)
                attend(blk, len(blk.rounds) - 1)
                if blk.last:
                    pe.wait_ge(exp_done, blk.before(7, 5) + len(blk.rounds))
                    pe.wait_ge(state_set, 1)
                    nc.tensor.transpose(aux[0:32, 1, 0:P], state[:, :], ident[:, :]).then_inc(state_t, 1)
                    sum_all2(0)
                    for h in range(8, 16):
                        out_half(blk, h)
                else:
                    transpose_x(nxt, 1)
                    out_half(blk, 8)
                    transpose_x(nxt, 2)
                    out_half(blk, 9)
                    transpose_x(nxt, 3)
                    for h in range(10, 16):
                        out_half(blk, h)

            first = Block1(0)
            transpose_x(first, 0)
            pe.wait_ge(vec_in, 9 * 16)
            nc.tensor.transpose(banks[4][:, 0:VROWS], vrows[:, :], ident[0:VROWS, 0:VROWS]).then_inc(vec_t, 1)
            transpose_x(first, 1)
            transpose_x(first, 2)
            mix_block(first)
            with pe.Fori(1, NB1) as b:
                mix_block(Block1(b))
            mix_block(Block1(NB1, last=True))

            def transpose_y(b, r, cs=range(KT), tail=False):
                rows = y_tiles(r, tail)[0]
                if cs[0] == 0 and r > (2 if tail else 0):
                    pe.wait_ge(yout_done, 1 + 4 * b + r - (2 if tail else 0))
                for c in cs:
                    last = nc.tensor.transpose(rows[:, c // 4, (c % 4) * P:(c % 4 + 1) * P], hcur[:, c, r * YR:(r + 1) * YR],
                                               ident[:, :])
                if cs[-1] == KT - 1:
                    last.then_inc(yT_ready, 1)

            def up(b, flush):
                for j in range(FT):
                    pe.wait_ge(w_lo_done, G1 + b * U2 + j + 1)
                    if j >= 2:
                        pe.wait_ge(relu_done, 32 * b + j - 1)
                    if j == 0:
                        for c in range(KT):
                            pe.wait_ge(hn_lo_done, 8 * b + c + 1)
                            last = product(banks[0][:, 0:B2], 0, (P, 0), lambda k: hn_hi[:, k, :], lambda k: hn_lo[:, k, :],
                                           [(c, c)], start=c == 0, stop=c == KT - 1)
                    else:
                        last = product(banks[j % 2][:, 0:B2], j % 2, (P, 0), lambda k: hn_hi[:, k, :], lambda k: hn_lo[:, k, :],
                                       [(c, c) for c in range(KT)])
                    last.then_inc(unit_done, 1)
                    if flush and j in (1, 4, 7, 10):
                        if j == 1:
                            pe.wait_ge(y_done, 8 * b)
                            pe.wait_ge(std2_done, b + 1)
                        transpose_y(b - 1, j // 3)

            def down(b, prepare):
                for m in range(32):
                    dp, kq, a = m // 8, (m % 8) // 2, m % 2
                    pe.wait_ge(w_lo_done, G1 + b * U2 + 32 + m + 1)
                    if dp == 0 and a == 0:
                        pe.wait_ge(hid_lo_done, 32 * b + 8 * (kq + 1))
                    if dp >= 2 and kq == 0:
                        pe.wait_ge(y_done, 8 * b + 2 * (dp - 2) + a + 1)
                    product(banks[2 + dp % 2 * 2 + a][:, 0:B2], m % 2, (P, 0), lambda k: hid_hi[:, k, :],
                            lambda k: hid_lo[:, k, :], [(c, kq * KT + c) for c in range(KT)],
                            start=kq == 0, stop=kq == 3).then_inc(unit_done, 1)
                    if prepare and m == 3:
                        pe.wait_ge(yout_done, 1 + 4 * b)
                        sum_all2(b + 1)
                    if not prepare and m == 28:
                        pe.wait_ge(y_done, 8 * b + 6)
                        pe.wait_ge(yout_done, 1 + 4 * b)
                        for r in range(3):
                            transpose_y(b, r, range(6), tail=True)

            pe.wait_ge(freed, 2 + (NB1 + 1) * USES)
            up(0, False)
            with pe.Fori(0, NB2 - 1) as b:
                down(b, True)
                up(b + 1, True)
            down(NB2 - 1, False)
            pe.wait_ge(y_done, 8 * NB2)
            for r in range(4):
                transpose_y(NB2 - 1, r, range(6, KT) if r < 3 else range(KT), tail=True)


_INS = ['x_prompt', 'x_sample', 'cache_k', 'cache_v', 'state_conv', 'state_lru', 'norm_mix_g', 'w_in', 'attn_sinks',
        'conv_w', 'conv_b', 'gate_a_w', 'gate_a_b', 'gate_x_w', 'gate_x_b', 'lru_lambda', 'w_out', 'norm_ffn_g',
        'w_up', 'w_down', 'final_norm_g']
_OUTS = [(1, SEQ, D), (1, SAMPLE, D), (1, 1, WINDOW, 2, HEAD), (1, 1, WINDOW, 2, HEAD), (1, 1, TAPS - 1, LRU), (1, 1, LRU),
         (1, 1, WINDOW, 2, HEAD), (1, 1, WINDOW, 2, HEAD), (1, 1, TAPS - 1, LRU), (1, 1, LRU)]


def kernel(**inputs):
    import concourse.bacc as bacc
    from concourse.bass_utils import run_bass_kernel_spmd

    nc = bacc.Bacc("TRN2", target_bir_lowering=False, num_devices=1)
    arrays, args = {}, []
    for name in _INS:
        a = np.ascontiguousarray(inputs[name])
        arrays[f"in_{name}"] = a
        args.append(nc.dram_tensor(f"in_{name}", a.shape, mybir.dt.from_np(a.dtype), kind="ExternalInput").ap())
    for i, shape in enumerate(_OUTS):
        args.append(nc.dram_tensor(f"out_{i}", shape, F32, kind="ExternalOutput").ap())
    build_program(nc, *args)
    r = run_bass_kernel_spmd(nc, [arrays], core_ids=[0])
    return tuple(r.results[0][f"out_{i}"] for i in range(len(_OUTS)))
```
